# Optimizing a Trainium2 kernel written in Bass

```python
import math
import jax, jax.numpy as jnp
from jax import lax
import numpy as np

D_MODEL = 1024
BATCH = 1
SEQ = 512
DEPTH = 2
DEC_BATCH = 1
DEC_SEQ = 256
PAST_LEN = 128

HEAD_DIM = 64
N_ATT_HEADS = 8
N_KV_HEADS = 2
ATT_WIDTH = N_ATT_HEADS * HEAD_DIM
KV_WIDTH = N_KV_HEADS * HEAD_DIM
WINDOW = 128
BLOCK = 128
ROT_DIM = HEAD_DIM // 4
ROPE_THETA = 500000.0
MLSTM_WIDTH = D_MODEL - ATT_WIDTH
N_MLSTM_HEADS = 4
MLSTM_HEAD_DIM = MLSTM_WIDTH // N_MLSTM_HEADS
CHUNK = 128
CONV_WIDTH = 3
MIX_WIDTH = ATT_WIDTH + MLSTM_WIDTH
OFF_AQ = 0
OFF_AK = OFF_AQ + ATT_WIDTH
OFF_AV = OFF_AK + KV_WIDTH
OFF_MQ = OFF_AV + KV_WIDTH
OFF_MK = OFF_MQ + MLSTM_WIDTH
OFF_MV = OFF_MK + MLSTM_WIDTH
OFF_MO = OFF_MV + MLSTM_WIDTH
OFF_G = OFF_MO + MLSTM_WIDTH
N_GATE_COLS = 4 * N_MLSTM_HEADS
IN_WIDTH = OFF_G + N_GATE_COLS
N_MEM = 256
N_X_HEADS = 4
X_HEAD_DIM = D_MODEL // N_X_HEADS
N_EXPERTS = 16
N_GROUPS = 4
EXPERTS_PER_GROUP = N_EXPERTS // N_GROUPS
TOP_K = 2
D_FF_EXPERT = 512
MOE_BLOCK = 128
ALPHA = (2.0 * DEPTH) ** 0.25
BETA = (8.0 * DEPTH) ** -0.25
LN_EPS = 1e-5
RMS_EPS = 1e-6
NEG = -1e30

kernel_name = 'hymba_swa_mlstm_shared_router_moe_encoder'

def layer_norm(x, g, b):
    xf = x.astype(jnp.float32)
    mu = jnp.mean(xf, axis=-1, keepdims=True)
    var = jnp.mean(jnp.square(xf - mu), axis=-1, keepdims=True)
    y = (xf - mu) * lax.rsqrt(var + LN_EPS) * g.astype(jnp.float32) + b.astype(jnp.float32)
    return y.astype(x.dtype)

def rms_norm(x, g):
    xf = x.astype(jnp.float32)
    return xf * lax.rsqrt(jnp.mean(jnp.square(xf), axis=-1, keepdims=True) + RMS_EPS) * g.astype(jnp.float32)

def partial_rope(x, pos):
    inv_freq = ROPE_THETA ** (-jnp.arange(0, ROT_DIM, 2, dtype=jnp.float32) / ROT_DIM)
    ang = pos.astype(jnp.float32)[:, None] * inv_freq[None, :]
    cos = jnp.cos(ang)[None, :, None, :]
    sin = jnp.sin(ang)[None, :, None, :]
    xr = x[..., :ROT_DIM].astype(jnp.float32)
    x1, x2 = xr[..., :ROT_DIM // 2], xr[..., ROT_DIM // 2:]
    rot = jnp.concatenate([x1 * cos - x2 * sin, x2 * cos + x1 * sin], axis=-1).astype(x.dtype)
    return jnp.concatenate([rot, x[..., ROT_DIM:]], axis=-1)

def windowed_gqa(q, k, v, sink):
    B, S = q.shape[0], q.shape[1]
    nb = S // BLOCK
    G = N_ATT_HEADS // N_KV_HEADS
    qb = q.reshape(B, nb, BLOCK, N_KV_HEADS, G, HEAD_DIM)

    def band(t):
        tp = jnp.pad(t.reshape(B, nb, BLOCK, N_KV_HEADS, HEAD_DIM), ((0, 0), (1, 1), (0, 0), (0, 0), (0, 0)))
        return jnp.concatenate([tp[:, :-2], tp[:, 1:-1], tp[:, 2:]], axis=2)

    kw, vw = band(k), band(v)
    s = jnp.einsum('bnqhgd,bnkhd->bnhgqk', qb, kw, preferred_element_type=jnp.float32) * (1.0 / math.sqrt(HEAD_DIM))
    q_off = jnp.arange(BLOCK)[:, None]
    k_off = jnp.arange(3 * BLOCK)[None, :] - BLOCK
    in_band = jnp.abs(k_off - q_off) <= WINDOW
    k_abs = jnp.arange(nb)[:, None] * BLOCK + k_off
    in_seq = (k_abs >= 0) & (k_abs < S)
    mask = in_band[None, :, :] & in_seq[:, None, :]
    s = jnp.where(mask[None, :, None, None], s, NEG)
    sink_l = sink.astype(jnp.float32).reshape(N_KV_HEADS, G)[None, None, :, :, None, None]
    m = jnp.maximum(jnp.max(s, axis=-1, keepdims=True), sink_l)
    p = jnp.exp(s - m)
    denom = jnp.sum(p, axis=-1, keepdims=True) + jnp.exp(sink_l - m)
    o = jnp.einsum('bnhgqk,bnkhd->bnqhgd', (p / denom).astype(v.dtype), vw)
    return o.reshape(B, S, ATT_WIDTH)

def mlstm_chunkwise(q, k, v, ig, lf):
    B, H, S, D = q.shape
    nc = S // CHUNK
    qc = q.reshape(B, H, nc, CHUNK, D)
    kc = k.reshape(B, H, nc, CHUNK, D)
    vc = v.reshape(B, H, nc, CHUNK, D)
    igc = ig.reshape(B, H, nc, CHUNK)
    b = jnp.cumsum(lf.reshape(B, H, nc, CHUNK), axis=-1)
    a = b[..., -1]
    w_log = a[..., None] - b + igc
    g = jnp.max(w_log, axis=-1)
    wk = jnp.exp(w_log - g[..., None])[..., None] * kc
    c_chunk = jnp.einsum('bhnld,bhnle->bhnde', wk, vc)
    n_chunk = jnp.sum(wk, axis=-2)

    def step(carry, inp):
        C, n, m = carry
        a_c, g_c, Cc, nc_ = inp
        m_new = jnp.maximum(a_c + m, g_c)
        f_s = jnp.exp(a_c + m - m_new)
        i_s = jnp.exp(g_c - m_new)
        C_new = f_s[..., None, None] * C + i_s[..., None, None] * Cc
        n_new = f_s[..., None] * n + i_s[..., None] * nc_
        return (C_new, n_new, m_new), (C, n, m)

    init = (jnp.zeros((B, H, D, D), jnp.float32), jnp.zeros((B, H, D), jnp.float32), jnp.zeros((B, H), jnp.float32))
    xs = (jnp.moveaxis(a, 2, 0), jnp.moveaxis(g, 2, 0), jnp.moveaxis(c_chunk, 2, 0), jnp.moveaxis(n_chunk, 2, 0))
    _, (C_in, n_in, m_in) = lax.scan(step, init, xs)
    C_in = jnp.moveaxis(C_in, 0, 2)
    n_in = jnp.moveaxis(n_in, 0, 2)
    m_in = jnp.moveaxis(m_in, 0, 2)
    causal = jnp.tril(jnp.ones((CHUNK, CHUNK), dtype=bool))
    log_d = jnp.where(causal, b[..., :, None] - b[..., None, :] + igc[..., None, :], NEG)
    inter_log = b + m_in[..., None]
    m_t = jnp.maximum(inter_log, jnp.max(log_d, axis=-1))
    dmat = jnp.exp(log_d - m_t[..., None])
    inter_w = jnp.exp(inter_log - m_t)
    sw = jnp.einsum('bhnld,bhnsd->bhnls', qc, kc) * dmat
    num = jnp.einsum('bhnls,bhnsd->bhnld', sw, vc) + inter_w[..., None] * jnp.einsum('bhnld,bhnde->bhnle', qc, C_in)
    den = jnp.sum(sw, axis=-1) + inter_w * jnp.einsum('bhnld,bhnd->bhnl', qc, n_in)
    h = num / jnp.maximum(jnp.abs(den), jnp.exp(-m_t))[..., None]
    return h.reshape(B, H, S, D)

def centred_dwconv(x, w, b):
    C = x.shape[-1]
    y = lax.conv_general_dilated(x, w.reshape(CONV_WIDTH, 1, C).astype(x.dtype), window_strides=(1,),
                                 padding=[(CONV_WIDTH // 2, CONV_WIDTH // 2)],
                                 dimension_numbers=('NWC', 'WIO', 'NWC'), feature_group_count=C)
    return y + b.astype(x.dtype)

def mlstm_group(u_qk, u_v, u_o, u_gates, conv_w, conv_b, gate_bias, norm_g):
    B, S = u_qk.shape[0], u_qk.shape[1]
    qk = jax.nn.silu(centred_dwconv(u_qk, conv_w, conv_b))

    def heads(t):
        return t.reshape(B, S, N_MLSTM_HEADS, MLSTM_HEAD_DIM).transpose(0, 2, 1, 3).astype(jnp.float32)

    q = heads(qk[..., :MLSTM_WIDTH])
    k = heads(qk[..., MLSTM_WIDTH:]) * (MLSTM_HEAD_DIM ** -0.5)
    v = heads(u_v)
    gts = (u_gates + gate_bias).astype(jnp.float32).transpose(0, 2, 1)
    i_f, f_f, i_b, f_b = jnp.split(gts, 4, axis=1)
    h_f = mlstm_chunkwise(q, k, v, i_f, jax.nn.log_sigmoid(f_f))
    fl = lambda t: jnp.flip(t, axis=2)
    h_b = fl(mlstm_chunkwise(fl(q), fl(k), fl(v), fl(i_b), fl(jax.nn.log_sigmoid(f_b))))
    h = (h_f + h_b).transpose(0, 2, 1, 3)
    h = rms_norm(h, norm_g.reshape(N_MLSTM_HEADS, MLSTM_HEAD_DIM)).reshape(B, S, MLSTM_WIDTH)
    return (h * jax.nn.sigmoid(u_o.astype(jnp.float32))).astype(u_o.dtype)

def parallel_mixer(x, pos, w_in, gate_bias, conv_w, conv_b, sink, att_g, mlstm_g, w_out):
    B, S, _ = x.shape
    u = x @ w_in
    aq = partial_rope(u[..., OFF_AQ:OFF_AK].reshape(B, S, N_ATT_HEADS, HEAD_DIM), pos)
    ak = partial_rope(u[..., OFF_AK:OFF_AV].reshape(B, S, N_KV_HEADS, HEAD_DIM), pos)
    av = u[..., OFF_AV:OFF_MQ].reshape(B, S, N_KV_HEADS, HEAD_DIM)
    y_att = rms_norm(windowed_gqa(aq, ak, av, sink), att_g).astype(x.dtype)
    y_ml = mlstm_group(u[..., OFF_MQ:OFF_MV], u[..., OFF_MV:OFF_MO], u[..., OFF_MO:OFF_G], u[..., OFF_G:],
                       conv_w, conv_b, gate_bias, mlstm_g)
    return jnp.concatenate([y_att, y_ml], axis=-1) @ w_out

def memory_cross_attention(x, mem, wq, wkv, wo):
    B, S, _ = x.shape
    M = mem.shape[1]
    q = (x @ wq).reshape(B, S, N_X_HEADS, X_HEAD_DIM)
    kv = mem @ wkv
    k = kv[..., :D_MODEL].reshape(B, M, N_X_HEADS, X_HEAD_DIM)
    v = kv[..., D_MODEL:].reshape(B, M, N_X_HEADS, X_HEAD_DIM)
    s = jnp.einsum('bqhd,bkhd->bhqk', q, k, preferred_element_type=jnp.float32) * (1.0 / math.sqrt(X_HEAD_DIM))
    p = jax.nn.softmax(s, axis=-1).astype(v.dtype)
    o = jnp.einsum('bhqk,bkhd->bqhd', p, v).reshape(B, S, D_MODEL)
    return o @ wo

def route(x2, router_w, router_bias):
    T = x2.shape[0]
    s = jax.nn.sigmoid((x2 @ router_w).astype(jnp.float32))
    sel = (s + router_bias.astype(jnp.float32)).reshape(T, N_GROUPS, EXPERTS_PER_GROUP)
    grp_score = jnp.sum(lax.top_k(sel, TOP_K)[0], axis=-1)
    g_idx = jnp.argmax(grp_score, axis=-1)
    in_group = jnp.take_along_axis(sel, g_idx[:, None, None], axis=1)[:, 0]
    _, local = lax.top_k(in_group, TOP_K)
    e_idx = (g_idx[:, None] * EXPERTS_PER_GROUP + local).astype(jnp.int32)
    w = jnp.take_along_axis(s, e_idx, axis=-1)
    return e_idx, w / jnp.sum(w, axis=-1, keepdims=True)

def grouped_moe(x, router_w, router_bias, w_gate, w_up, w_down):
    B, S, D = x.shape
    T = B * S
    x2 = x.reshape(T, D)
    e_idx, gw = route(x2, router_w, router_bias)
    A = T * TOP_K
    flat_e = e_idx.reshape(A)
    flat_tok = jnp.arange(A, dtype=jnp.int32) // TOP_K
    order = jnp.argsort(flat_e)
    sorted_e = flat_e[order]
    sorted_tok = flat_tok[order]
    counts = jnp.bincount(flat_e, length=N_EXPERTS).astype(jnp.int32)
    padded = (counts + MOE_BLOCK - 1) // MOE_BLOCK * MOE_BLOCK
    pad_end = jnp.cumsum(padded)
    pad_start = pad_end - padded
    start = jnp.cumsum(counts) - counts
    dest = pad_start[sorted_e] + jnp.arange(A, dtype=jnp.int32) - start[sorted_e]
    P = A + N_EXPERTS * MOE_BLOCK
    n_blk = P // MOE_BLOCK
    slot_tok = jnp.full((P,), T, dtype=jnp.int32).at[dest].set(sorted_tok)
    xp = jnp.concatenate([x2, jnp.zeros((1, D), x2.dtype)], axis=0)[slot_tok]
    blk_e = jnp.minimum(jnp.searchsorted(pad_end, jnp.arange(n_blk, dtype=jnp.int32) * MOE_BLOCK, side='right'),
                        N_EXPERTS - 1).astype(jnp.int32)

    def expert_block(args):
        xb, e = args
        h = jax.nn.silu(xb @ w_gate[e]) * (xb @ w_up[e])
        return h @ w_down[e]

    yp = lax.map(expert_block, (xp.reshape(n_blk, MOE_BLOCK, D), blk_e)).reshape(P, D)
    y_assign = yp[dest] * gw.reshape(A)[order][:, None].astype(yp.dtype)
    y = jax.ops.segment_sum(y_assign, sorted_tok, num_segments=T)
    return y.reshape(B, S, D)

def trunk(x, mem, weights):
    (w_in, gate_bias, conv_w, conv_b, attn_sink, attn_norm_g, mlstm_norm_g, w_out, ln1_g, ln1_b,
     wq_mem, wkv_mem, wo_mem, ln2_g, ln2_b, router_w, router_bias, w_gate, w_up, w_down, ln3_g, ln3_b) = weights
    pos = jnp.arange(x.shape[1], dtype=jnp.int32)
    for l in range(DEPTH):
        y = parallel_mixer(x, pos, w_in[l], gate_bias[l], conv_w[l], conv_b[l], attn_sink[l],
                           attn_norm_g[l], mlstm_norm_g[l], w_out[l])
        x = layer_norm(ALPHA * x + y, ln1_g[l], ln1_b[l])
        y = memory_cross_attention(x, mem, wq_mem[l], wkv_mem[l], wo_mem[l])
        x = layer_norm(ALPHA * x + y, ln2_g[l], ln2_b[l])
        y = grouped_moe(x, router_w, router_bias, w_gate[l], w_up[l], w_down[l])
        x = layer_norm(ALPHA * x + y, ln3_g[l], ln3_b[l])
    return x

def setup_inputs(seed: int = 0) -> dict:
    key = jax.random.key(seed)
    ks = jax.random.split(key, 32)
    f32 = jnp.float32
    nrm = lambda k, shape, scale: jax.random.normal(k, shape, f32) * scale
    ig_b = nrm(ks[4], (DEPTH, 2, 1, N_MLSTM_HEADS), 0.1)
    fg_b = jnp.linspace(3.0, 6.0, N_MLSTM_HEADS, dtype=f32)[None, None, None, :] + nrm(ks[5], (DEPTH, 2, 1, N_MLSTM_HEADS), 0.1)
    gate_bias = jnp.concatenate([ig_b, fg_b], axis=2).reshape(DEPTH, N_GATE_COLS)
    return {
        'x_prompt': nrm(ks[0], (BATCH, SEQ, D_MODEL), 1.0),
        'x_sample': nrm(ks[1], (DEC_BATCH, DEC_SEQ, D_MODEL), 1.0),
        'mem_prompt': nrm(ks[2], (BATCH, N_MEM, D_MODEL), 1.0),
        'mem_sample': nrm(ks[3], (DEC_BATCH, N_MEM, D_MODEL), 1.0),
        'w_in': nrm(ks[6], (DEPTH, D_MODEL, IN_WIDTH), D_MODEL ** -0.5),
        'gate_bias': gate_bias,
        'conv_w': nrm(ks[7], (DEPTH, CONV_WIDTH, 2 * MLSTM_WIDTH), CONV_WIDTH ** -0.5),
        'conv_b': nrm(ks[8], (DEPTH, 2 * MLSTM_WIDTH), 0.02),
        'attn_sink': nrm(ks[9], (DEPTH, N_ATT_HEADS), 0.5),
        'attn_norm_g': 1.0 + nrm(ks[10], (DEPTH, ATT_WIDTH), 0.02),
        'mlstm_norm_g': 1.0 + nrm(ks[11], (DEPTH, MLSTM_WIDTH), 0.02),
        'w_out': nrm(ks[12], (DEPTH, MIX_WIDTH, D_MODEL), MIX_WIDTH ** -0.5 * BETA),
        'ln1_g': 1.0 + nrm(ks[13], (DEPTH, D_MODEL), 0.02),
        'ln1_b': nrm(ks[14], (DEPTH, D_MODEL), 0.02),
        'wq_mem': nrm(ks[15], (DEPTH, D_MODEL, D_MODEL), D_MODEL ** -0.5),
        'wkv_mem': nrm(ks[16], (DEPTH, D_MODEL, 2 * D_MODEL), D_MODEL ** -0.5),
        'wo_mem': nrm(ks[17], (DEPTH, D_MODEL, D_MODEL), D_MODEL ** -0.5 * BETA),
        'ln2_g': 1.0 + nrm(ks[18], (DEPTH, D_MODEL), 0.02),
        'ln2_b': nrm(ks[19], (DEPTH, D_MODEL), 0.02),
        'router_w': nrm(ks[20], (D_MODEL, N_EXPERTS), D_MODEL ** -0.5),
        'router_bias': nrm(ks[21], (N_EXPERTS,), 0.01),
        'w_gate': nrm(ks[22], (DEPTH, N_EXPERTS, D_MODEL, D_FF_EXPERT), D_MODEL ** -0.5),
        'w_up': nrm(ks[23], (DEPTH, N_EXPERTS, D_MODEL, D_FF_EXPERT), D_MODEL ** -0.5),
        'w_down': nrm(ks[24], (DEPTH, N_EXPERTS, D_FF_EXPERT, D_MODEL), D_FF_EXPERT ** -0.5 * BETA),
        'ln3_g': 1.0 + nrm(ks[25], (DEPTH, D_MODEL), 0.02),
        'ln3_b': nrm(ks[26], (DEPTH, D_MODEL), 0.02),
    }

def reference(x_prompt, x_sample, mem_prompt, mem_sample, w_in, gate_bias, conv_w, conv_b, attn_sink,
              attn_norm_g, mlstm_norm_g, w_out, ln1_g, ln1_b, wq_mem, wkv_mem, wo_mem, ln2_g, ln2_b,
              router_w, router_bias, w_gate, w_up, w_down, ln3_g, ln3_b):
    weights = (w_in, gate_bias, conv_w, conv_b, attn_sink, attn_norm_g, mlstm_norm_g, w_out, ln1_g, ln1_b,
               wq_mem, wkv_mem, wo_mem, ln2_g, ln2_b, router_w, router_bias, w_gate, w_up, w_down, ln3_g, ln3_b)
    y_prompt = trunk(x_prompt, mem_prompt, weights)
    y_sample = trunk(x_sample, mem_sample, weights)
    return (y_prompt, y_sample)


_drawn_inputs = setup_inputs


def setup_inputs(seed=0):
    import zlib

    import numpy as np

    out = dict(_drawn_inputs(seed))
    spreads = {}
    factors = {'conv_b': 5.183, 'attn_sink': 5.714, 'mlstm_norm_g': 4.483}
    for name, (base, spread) in spreads.items():
        noise = np.random.default_rng([zlib.crc32(name.encode()), seed]).standard_normal(out[name].shape)
        drawn = base * np.exp(spread * noise) if base else spread * noise
        out[name] = __import__('jax').numpy.asarray(drawn.astype(out[name].dtype))
    for name, factor in factors.items():
        out[name] = (out[name] * factor).astype(out[name].dtype)
    return out
```

```python
from contextlib import ExitStack

import numpy as np

import concourse.bass as bass
from concourse import mybir

F32 = mybir.dt.float32
I32 = mybir.dt.int32
U32 = mybir.dt.uint32
ALU = mybir.AluOpType
ACT = mybir.ActivationFunctionType
AX = mybir.AxisListType

P = 128
DEPTH = 2
D = 1024
KD = D // P
SEQS = (512, 256)
T = sum(SEQS)
NC = T // P
CHUNKS = tuple(n // P for n in SEQS)
BASE = (0, CHUNKS[0])
SEQ_OF = tuple(s for s in range(2) for _ in range(CHUNKS[s]))
HD = 64
NH = 8
NKV = 2
GRP = NH // NKV
ATT = NH * HD
MH = 4
MD = 128
ML = MH * MD
ROT = HD // 4
HALF = ROT // 2
IN_W = 2832
OFF_K, OFF_MQ, OFF_MK, OFF_MV, OFF_MO, OFF_G = 512, 768, 1280, 1792, 2304, 2816
NG = 16
NMEM = 256
MC = NMEM // P
XH = 4
XD = D // XH
NE = 16
GROUPS = 4
EPG = NE // GROUPS
FF = 512
BLOCKS = (2 * T - NE) // P + NE
XBLOCKS = BLOCKS + 1
ALPHA = (2.0 * DEPTH) ** 0.25
NEG = -1e30
SLOTS = 3
FAR = 1.0e6

C_ID, C_STRICT, C_ONES, C_MASK = 0, 128, 256, 384
C_TRI = 768
C_SEL = C_TRI + EPG * EPG
C_COS = C_SEL + 8 * P
C_SIN = C_COS + NC * HALF
C_FWD = C_SIN + NC * HALF
C_BWD, C_EPS_LN, C_EPS_RMS, C_ONE = C_FWD + 1, C_FWD + 2, C_FWD + 3, C_FWD + 4
C_STEP = C_FWD + 5
C_IOTA = C_STEP + NC
C_ALL = C_IOTA + XBLOCKS

M_QT, M_KT, M_KV, M_CONV = 0, 3072, 3840, 5376
M_V = M_CONV + 8 * T
M_ALL = M_V + NC * MH * (MD + 1)
SW_DIR = 1280
X_VM, X_MEMT = 0, M_CONV
X_KM = X_MEMT + KD * 2 * NMEM
X_P, X_PT = M_CONV, M_CONV + 1024
Z_S, Z_PT = 0, GRP * 384
Z_D, Z_R, Z_H = 0, 1024, 2048
Z_ALL = 3080


def constants():
    c = np.zeros((P, C_ALL), np.float32)
    p = np.arange(P)
    c[:, C_ID:C_ID + P] = np.eye(P)
    c[:, C_STRICT:C_STRICT + P] = p[:, None] < p[None, :]
    c[:, C_ONES:C_ONES + P] = 1.0
    c[:, C_MASK:C_MASK + P] = np.where(p[None, :] >= p[:, None], 0.0, NEG)
    c[:, C_MASK + 2 * P:C_MASK + 3 * P] = np.where(p[None, :] <= p[:, None], 0.0, NEG)
    c[:, C_TRI:C_TRI + EPG * EPG] = [float(j < i) for i in range(EPG) for j in range(EPG)]
    for r in range(8):
        c[r, C_SEL + r * P:C_SEL + (r + 1) * P] = 1.0
    inv = np.float32(500000.0) ** (-np.arange(0, ROT, 2, dtype=np.float32) / np.float32(ROT))
    for ch in range(NC):
        pos = (p + P * (ch - BASE[SEQ_OF[ch]])).astype(np.float32)
        ang = pos[:, None] * inv[None, :].astype(np.float32)
        c[:, C_COS + ch * HALF:C_COS + (ch + 1) * HALF] = np.cos(ang)
        c[:, C_SIN + ch * HALF:C_SIN + (ch + 1) * HALF] = np.sin(ang)
    c[0:4, C_FWD] = 1.0
    c[4:8, C_BWD] = 1.0
    c[:, C_EPS_LN], c[:, C_EPS_RMS], c[:, C_ONE] = 1e-5, 1e-6, 1.0
    c[:, C_STEP:C_STEP + NC] = P * np.arange(NC)
    c[:, C_IOTA:C_IOTA + XBLOCKS] = np.arange(XBLOCKS)
    return c


GROUP_ORDER = [(c, n) for c in range(NC) for n in range(NKV)]
STREAM = ([("cv", 4 + j, s) for j in range(4) for s in range(2)] + [("cv", j, s) for j in range(4) for s in range(2)]
          + [("v", c) for c in range(NC)] + [("o", c) for c in range(NC)])
PER_SLOT = [3, 2, 2, 3, 2, 2, 3, 2, 2, 3, 2, 2]
STARTS = [sum(PER_SLOT[:i]) for i in range(13)]
ML_GROUPS = [(h, s) for h in range(MH) for s in range(2)]
X_ITEMS = [(c, hp) for c in range(NC) for hp in range(2)]


def slot_tiles(i):
    return STREAM[STARTS[i]:STARTS[i + 1]] if i < 12 else []


def keys_of(c):
    s = SEQ_OF[c]
    lo, hi = max(c - 1, BASE[s]), min(c + 1, BASE[s] + CHUNKS[s] - 1)
    return lo, hi - lo + 1, (lo - c + 1) * P


def tile_plan():
    place, used, turn = {}, [0] * 8, {}

    def add(key, banks):
        b = banks[turn.get(banks, 0) % len(banks)]
        turn[banks] = turn.get(banks, 0) + 1
        place[key] = (b, used[b])
        used[b] += 1

    every = tuple(range(8))
    for c in range(NC):
        add(("kvg", c), every)
    for c in range(NC):
        add(("q", c), every)
    for k in ("gi", "gf", "gs", "kt0", "kt1"):
        add((k,), every)
    for c in range(NC):
        add(("qt", c), every)
    add(("cw",), every)
    add(("zt",), every)
    for i in range(13):
        w = slot_tiles(i)
        if i:
            add(("pt", i - 1, 0), (4, 5))
            add(("pt", i - 1, 1), (4, 5))
        if w:
            add(w[0], (6, 7))
        if i:
            add(("pt", i - 1, 2), (4, 5))
            add(("pt", i - 1, 3), (4, 5))
        if i < 12:
            for j in range(GRP):
                add(("sc", i, j), (0, 1, 2, 3))
        for t in w[1:]:
            add(t, (6, 7))
        if i:
            add(("pv", i - 1), (4, 5))
    for c in range(NC):
        add(("yt", c, 0), (4, 5, 6, 7))
    for g in range(9):
        if g < 8:
            add(("rb", g, 0), (0, 1))
            add(("rb", g, 1), (0, 1))
            for s in range(CHUNKS[ML_GROUPS[g][1]]):
                add(("st", g, s), (2, 3, 4))
        if g:
            for t in range(CHUNKS[ML_GROUPS[g - 1][1]]):
                add(("nm", g - 1, t), (5, 6, 7))
    for c in range(NC):
        add(("yt", c, 1), every)
    for c in range(NC):
        for h in range(2):
            add(("wo", c, h), every)
    for k in range(KD):
        add(("mt", k), every)
    for j in range(KD):
        add(("km", j), every)
    for m in range(2 * MC):
        for h in range(2):
            add(("vm", m, h), every)
    for c in range(NC):
        for h in range(2):
            add(("x2", c, h), every)
    for j in range(KD):
        for s in range(2):
            add(("qx", j, s), every)
    add(("sx", 0), (0, 1, 2))
    for i in range(12):
        if i + 1 < 12:
            add(("sx", i + 1), (0, 1, 2))
        add(("px", i), (3, 4))
        if i % 4 == 3:
            for m in range(4):
                add(("ox", i // 4, m), (3, 4))
            if i // 4:
                for c in (2 * (i // 4) - 2, 2 * (i // 4) - 1):
                    for h in range(2):
                        add(("wx", c, h), (5, 6, 7))
    for c in (4, 5):
        for h in range(2):
            add(("wx", c, h), (5, 6, 7))
    for c in range(NC):
        for h in range(2):
            add(("x3", c, h), (0, 1, 2, 3))
        if c == NC - 1:
            add(("rt",), (4,))
    add(("rank",), (5,))
    before_experts = list(used)
    for c in range(NC):
        for h in range(2):
            add(("xn", c, h), every)
    return place, before_experts


TILES, USES_BEFORE_EXPERTS = tile_plan()

UNITS = [
    ("kvg", ("kvg", NC - 1)), ("q", ("q", NC - 1)), ("mk", ("cv", 7, 1)), ("mq", ("cv", 3, 1)),
    ("mv", ("v", NC - 1)), ("mo", ("o", NC - 1)), ("wo0", ("wo", NC - 1, 1)), ("wo1", ("wo", NC - 1, 1)),
    ("mem", ("mt", KD - 1)), ("wk0", ("km", 3)), ("wk1", ("km", KD - 1)), ("wv0", ("vm", 2 * MC - 1, 1)),
    ("wv1", ("vm", 2 * MC - 1, 1)), ("wq0", ("qx", 3, 1)), ("wq1", ("qx", KD - 1, 1)),
    ("wx0", ("wx", NC - 1, 1)), ("wx1", ("wx", NC - 1, 1)),
]
UNIT = {name: n for n, (name, _) in enumerate(UNITS)}
AHEAD = SLOTS
assert DEPTH == 2 and [name for name, _ in UNITS[:AHEAD]] == ["kvg", "q", "mk"]


def build_program(nc, x_prompt, x_sample, mem_prompt, mem_sample, w_in, gate_bias, conv_w, conv_b, attn_sink,
                  attn_norm_g, mlstm_norm_g, w_out, ln1_g, ln1_b, wq_mem, wkv_mem, wo_mem, ln2_g, ln2_b,
                  router_w, router_bias, w_gate, w_up, w_down, ln3_g, ln3_b, consts, y_prompt, y_sample,
                  stop_after=None):
    slots_x = nc.dram_tensor("slots_x", [XBLOCKS * P, D], F32).ap()
    slots_y = nc.dram_tensor("slots_y", [XBLOCKS * P, D], F32).ap()

    with ExitStack() as ctx:
        def sb(name, cols, dt=F32):
            return ctx.enter_context(nc.sbuf_tensor(name, [P, cols], dt))

        def sem(name):
            s = ctx.enter_context(nc.semaphore(name))
            return s

        layer_sems = []

        def lsem(name):
            s = sem(name)
            layer_sems.append(s)
            return s

        banks = [ctx.enter_context(nc.psum_tensor(f"bank{i}", [P, 512], F32)) for i in range(8)]

        x_t = sb("x", NC * D)
        x = x_t[:, :].rearrange("p (c d) -> p c d", c=NC)
        xt_t = sb("x_transposed", KD * T)
        xT = xt_t[:, :].rearrange("p (k t) -> p k t", k=KD)
        ring = sb("weight_slots", SLOTS * 4096)
        y_t = sb("mixed", NC * D)
        y = y_t[:, :].rearrange("p (c d) -> p c d", c=NC)
        qx = y_t[:, :].rearrange("p (k t) -> p k t", k=KD)
        mix = sb("mixer_region", M_ALL)
        z = sb("scratch", Z_ALL)
        rrow = sb("running_max_rows", T)
        cst = sb("constants", C_ALL)
        gmix = sb("mixer_norm_gains", D)
        esc = sb("silu_exp", 512)
        gts = sb("gates", NC * NG)
        gbias = sb("gate_bias_rows", NG)
        sink = sb("sink_rows", NH)
        rw_t = sb("router_weights", KD * NE)
        rbias = sb("router_bias_rows", NE)
        zn = sb("z_by_token", NC * 8)
        thr = sb("floor_by_token", NC * 8)
        cwb = sb("conv_taps", 32)
        st = sb("small", 120)

        ident = cst[:, C_ID:C_ID + P]
        eps_ln = cst[:, C_EPS_LN:C_EPS_LN + 1]
        eps_rms = cst[:, C_EPS_RMS:C_EPS_RMS + 1]
        one = cst[:, C_ONE:C_ONE + 1]

        def unit_view(name, cols, k=KD):
            s = UNIT[name] % SLOTS
            return ring[:, s * 4096:s * 4096 + k * cols].rearrange("p (k n) -> p k n", k=k)

        qT = mix[:, M_QT:M_QT + GRP * T].rearrange("p (j t) -> p j t", j=GRP)
        kT = mix[:, M_KT:M_KT + T]
        kv = mix[:, M_KV:M_KV + NC * 256].rearrange("p (c n) -> p c n", c=NC)
        conv = mix[:, M_CONV:M_CONV + 8 * T].rearrange("p (j t) -> p j t", j=8)
        va = mix[:, M_V:M_ALL].rearrange("p (c h d) -> p c h d", c=NC, h=MH)
        rows = mix[0:8, M_CONV:M_CONV + 8 * T].rearrange("p (j t) -> p j t", j=8)
        vm = mix[:, X_VM:X_VM + 4096].rearrange("p (m n) -> p m n", m=2 * MC)
        memT = mix[:, X_MEMT:X_MEMT + 4096].rearrange("p (k m) -> p k m", k=KD)
        km = mix[:, X_KM:X_KM + 4096].rearrange("p (k m) -> p k m", k=KD)
        xp = mix[:, X_P:X_P + 1024].rearrange("p (b n) -> p b n", b=2)
        xpt = mix[:, X_PT:X_PT + 2048].rearrange("p (h m t) -> p h m t", h=XH, m=MC)
        probs = z[:, Z_S:Z_S + GRP * 384].rearrange("p (j n) -> p j n", j=GRP)
        ptb = z[:, Z_PT:Z_PT + GRP * 384].rearrange("p (j n) -> p j n", j=GRP)
        dec = z[:, Z_D:Z_D + 1024].rearrange("p (b n) -> p b n", b=2)
        rbc = z[:, Z_R:Z_R + 1024].rearrange("p (b n) -> p b n", b=2)
        hsc = z[:, Z_H:Z_H + 1024].rearrange("p (b c d) -> p b c d", b=2, c=4)
        lng = z[:, 0:D]
        lnb = z[:, D:2 * D]
        xb = xt_t[:, 0:1024]
        xbT = xt_t[:, 1024:2048].rearrange("p (k t) -> p k t", k=KD)
        gact = xt_t[:, 2048:2560]
        hb = xt_t[:, 2560:3072]
        hbT = xt_t[:, 3072:3584].rearrange("p (k t) -> p k t", k=4)
        yb = xt_t[:, 3584:4608]
        zero_rows = y[:, NC - 1, ATT:D]
        r_at = [0]

        def rt(n, dt=F32):
            a = y_t[:, r_at[0]:r_at[0] + n]
            r_at[0] += n
            return a if dt == F32 else a.bitcast(dt)

        NS_ = NC * NE
        r_s, r_sel, r_gs, r_m, r_w, r_t1, r_t2 = rt(NS_), rt(NS_), rt(24), rt(NS_), rt(NS_), rt(NS_), rt(NS_)
        r_beat, r_beat2 = rt(384), rt(384)
        r_rank, r_gr, r_sum = rt(NS_), rt(24), rt(NC)
        r_tot, r_cnt, r_nb, r_end, r_start, r_slot = rt(NS_), rt(NE), rt(NE), rt(NE), rt(NE), rt(NS_)
        r_cmp, r_be, r_bei = rt(XBLOCKS * NE), rt(XBLOCKS), rt(XBLOCKS, I32)
        r_nbi = rt(1, I32)
        r_slots, gw = rt(2 * NC), rt(2 * NC)
        slot_ids = rt(2 * NC, I32)
        gath = mix[:, 0:2 * NC * D].rearrange("p (a c d) -> p a c d", a=2, c=NC)

        scattered = sem("slots_scattered")
        gathered = [sem(f"outputs_gathered{c}") for c in range(NC)]
        consts_loaded = sem("constants_loaded")
        x_in = [sem(f"x_loaded{i}") for i in range(3)]
        router_loaded = sem("router_loaded")
        ahead = [sem(f"unit_loaded_ahead{n}") for n in range(AHEAD)]
        start_turned = sem("x_turned")
        start_left = sem("x_left_taken")
        start_right = sem("x_right_taken")
        zeros_made = sem("zeros_made")
        zeros_stored = sem("zeros_stored")
        out_stored = sem("out_stored")
        filled = [lsem(f"filled{b}") for b in range(8)]
        drained = [lsem(f"drained{b}") for b in range(8)]
        unit_loaded = [lsem(f"unit_loaded{s}") for s in range(SLOTS)]
        rows_loaded = lsem("layer_rows_loaded")
        taps_loaded = lsem("conv_taps_loaded")
        ln_rows_loaded = [lsem(f"ln_rows_loaded{i}") for i in range(3)]
        dve_done = lsem("dve_step_done")
        act_done = lsem("act_step_done")
        ones_made = lsem("value_ones_made")
        gates_ready = lsem("gates_ready")
        lf_part = lsem("log_forget_parts")
        z_ready = lsem("z_rows_ready")
        k_roped = lsem("k_roped")
        q_roped = lsem("q_roped")
        s_masked = lsem("scores_masked")
        m_ready = lsem("row_max_ready")
        p_ready = lsem("probs_ready")
        cv_exp = lsem("conv_exp_ready")
        cv_used = lsem("conv_exp_used")
        o_exp = lsem("o_exp_ready")
        att_rs = lsem("attention_rms_ready")
        y_att = lsem("attention_half_ready")
        d_exp = lsem("decay_ready")
        d_masked = lsem("decay_masked")
        sw_ready = lsem("weights_ready")
        h_rs = lsem("h_rms_ready")
        y_ml = lsem("mlstm_half_ready")
        ln_var = lsem("ln_variance_ready")
        ln_rstd = lsem("ln_rstd_ready")
        x_ready = lsem("x_ready")
        xm_ready = lsem("cross_max_ready")
        xe_ready = lsem("cross_exp_ready")
        xp_ready = lsem("cross_probs_ready")
        mask_ready = lsem("expert_mask_ready")
        ids_ready = lsem("slot_ids_ready")
        x_loaded = lsem("block_x_loaded")
        g_loaded = lsem("gate_weights_loaded")
        u_loaded = lsem("up_weights_loaded")
        d_loaded = lsem("down_weights_loaded")
        xT_filled = lsem("block_xT_filled")
        xT_ready = lsem("block_xT_ready")
        g_filled = lsem("block_gate_filled")
        g_ready = lsem("block_silu_ready")
        u_filled = lsem("block_up_filled")
        h_done = lsem("block_h_ready")
        hT_filled = lsem("block_hT_filled")
        hT_ready = lsem("block_hT_ready")
        y_filled = lsem("block_y_filled")
        yl_ready = lsem("block_y_left_ready")
        yr_ready = lsem("block_y_right_ready")
        y_stored = lsem("block_y_stored")
        all_stored = lsem("all_blocks_stored")
        comb = lsem("combined")

        def tile_filled(eng, key):
            b, use = TILES[key]
            eng.wait_ge(filled[b], use + 1)

        def tile_drained(eng, key):
            b, use = TILES[key]
            eng.wait_ge(drained[b], use + 1)

        def bank_of(key):
            return banks[TILES[key][0]]

        def drain_sem(key):
            return drained[TILES[key][0]]

        def sw_at(g, d, n, sc, lo, hi):
            if d == 0:
                o = sum(n - q for q in range(sc)) + lo - sc
            else:
                o = sum(q + 1 for q in range(sc)) + lo
            o = (g % 2) * 2 * SW_DIR + d * SW_DIR + o * P
            return mix[:, o:o + (hi - lo) * P]

        def sel_rows(r):
            return cst[0:8, C_SEL + r * P:C_SEL + (r + 1) * P]

        def load_ahead(sp, layer):
            src = w_in[layer].rearrange("(k p) n -> p k n", p=P)
            v = unit_view("kvg", 272)
            sp.dma_start(v[:, :, 0:256], src[:, :, OFF_K:OFF_K + 256]).then_inc(ahead[0], 16)
            sp.dma_start(v[:, :, 256:272], src[:, :, OFF_G:OFF_G + NG]).then_inc(ahead[0], 16)
            for n, off in ((1, 0), (2, OFF_MK)):
                v = unit_view(UNITS[n][0], 512)
                for h in range(2):
                    sp.dma_start(v[:, 4 * h:4 * h + 4, :], src[:, 4 * h:4 * h + 4, off:off + 512]).then_inc(ahead[n], 16)

        X_PARTS = ((0, 2), (2, 2), (4, 2))
        with nc.Block() as start:
            @start.sync
            def _(sp):
                sp.dma_start(cst[:, :], consts).then_inc(consts_loaded, 16)
                xp_src = x_prompt[0].rearrange("(c p) d -> p c d", p=P)
                for i, src in enumerate((xp_src[:, 0:2, :], xp_src[:, 2:4, :], x_sample[0].rearrange("(c p) d -> p c d", p=P))):
                    sp.dma_start(x[:, 2 * i:2 * i + 2, :], src).then_inc(x_in[i], 16)
                load_ahead(sp, 0)
                sp.dma_start(rw_t[:, :].rearrange("p (k e) -> p k e", k=KD),
                             router_w.rearrange("(k p) e -> p k e", p=P)).then_inc(router_loaded, 16)
                sp.dma_start(rbias[:, :], router_bias.partition_broadcast(P)).then_inc(router_loaded, 16)

            @start.gpsimd
            def _(pool):
                nc.gpsimd.memset(zero_rows, 0.0).then_inc(zeros_made, 1)

            @start.tensor
            def _(pe):
                pe.wait_ge(consts_loaded, 16)
                for c in range(NC):
                    if c % 2 == 0:
                        pe.wait_ge(x_in[c // 2], 16)
                    for h in range(2):
                        if c >= 4:
                            pe.wait_ge((start_left, start_right)[h], c - 3)
                        for k in range(4):
                            ins = pe.transpose(banks[2 * (c % 4) + h][:, k * P:(k + 1) * P],
                                               x[:, c, (4 * h + k) * P:(4 * h + k + 1) * P], ident)
                        ins.then_inc(start_turned, 1)

            @start.scalar
            def _(act):
                for c in range(NC):
                    act.wait_ge(start_turned, 2 * c + 1)
                    nc.scalar.activation(xT[:, 0:4, c * P:(c + 1) * P],
                                         banks[2 * (c % 4)][:, :].rearrange("p (k t) -> p k t", k=4), ACT.Copy).then_inc(start_left, 1)

            @start.vector
            def _(dve):
                for c in range(NC):
                    dve.wait_ge(start_turned, 2 * c + 2)
                    nc.vector.tensor_copy(xT[:, 4:8, c * P:(c + 1) * P],
                                          banks[2 * (c % 4) + 1][:, :].rearrange("p (k t) -> p k t", k=4)).then_inc(start_right, 1)

        with nc.Fori(0, DEPTH) as l:
            with nc.Block() as block:
                @block.sync
                def _(sp):
                    def load_unit(name, last, n):
                        s = n % SLOTS
                        tile_filled(sp, UNITS[n - SLOTS][1])
                        if name == "mem":
                            v = ring[:, s * 4096:(s + 1) * 4096].rearrange("p (m d) -> p m d", m=2 * MC)
                            sp.dma_start(v[:, 0:MC, :], mem_prompt[0].rearrange("(m p) d -> p m d", p=P)).then_inc(unit_loaded[s], 16)
                            sp.dma_start(v[:, MC:2 * MC, :], mem_sample[0].rearrange("(m p) d -> p m d", p=P)).then_inc(unit_loaded[s], 16)
                            return
                        w, off = {"mq": (w_in, OFF_MQ), "mv": (w_in, OFF_MV),
                                  "mo": (w_in, OFF_MO), "wo0": (w_out, 0), "wo1": (w_out, 512), "wk0": (wkv_mem, 0),
                                  "wk1": (wkv_mem, 512), "wv0": (wkv_mem, 1024), "wv1": (wkv_mem, 1536),
                                  "wq0": (wq_mem, 0), "wq1": (wq_mem, 512), "wx0": (wo_mem, 0), "wx1": (wo_mem, 512)}[name]
                        src = w[l].rearrange("(k p) n -> p k n", p=P)[:, :, off:off + 512]
                        v = unit_view(name, 512)
                        for h in range(2):
                            sp.dma_start(v[:, 4 * h:4 * h + 4, :], src[:, 4 * h:4 * h + 4, :]).then_inc(unit_loaded[s], 16)

                    for n, (name, last) in enumerate(UNITS[AHEAD:], AHEAD):
                        load_unit(name, last, n)
                        if n == AHEAD + 1:
                            sp.wait_ge(zeros_made, 1)
                            with sp.If(l < 1):
                                for slots in (slots_x, slots_y):
                                    for h in range(2):
                                        sp.dma_start(slots.rearrange("(b p) (h d) -> p b h d", p=P, h=2)[:, :, h, :],
                                                     zero_rows.unsqueeze(1).broadcast_to([P, XBLOCKS, 512])).then_inc(zeros_stored, 16)

                    sp.wait_ge(ids_ready, 1)
                    n_blocks = sp.value_load(r_nbi[0:1, 0:1], min_val=1, max_val=BLOCKS)
                    tile_filled(sp, UNITS[-1][1])
                    sp.wait_ge(scattered, l * (16 * 2 * NC) + 16 * 2 * NC)
                    sp.dma_start(xb, slots_x[0:P, :]).then_inc(x_loaded, 16)
                    gs, us, ds = 2, 0, 1
                    with sp.Fori(0, n_blocks) as b:
                        e = sp.value_load(r_bei[0:1, bass.ds(b, 1)], min_val=0, max_val=NE - 1)
                        wv = ring[:, gs * 4096:(gs + 1) * 4096].rearrange("p (k n) -> p k n", k=KD)
                        sp.wait_ge(g_filled, b + 1)
                        sp.dma_start(wv, w_gate[l, e].rearrange("(k p) n -> p k n", p=P)).then_inc(g_loaded, 16)
                        wv = ring[:, us * 4096:(us + 1) * 4096].rearrange("p (k n) -> p k n", k=KD)
                        sp.wait_ge(u_filled, b + 1)
                        sp.dma_start(wv, w_up[l, e].rearrange("(k p) n -> p k n", p=P)).then_inc(u_loaded, 16)
                        sp.wait_ge(xT_filled, 2 * b + 2)
                        sp.dma_start(xb, slots_x.rearrange("(b p) d -> b p d", p=P)[b + 1]).then_inc(x_loaded, 16)
                        wv = ring[:, ds * 4096:(ds + 1) * 4096].rearrange("p (k n) -> p k n", k=4)
                        sp.wait_ge(y_filled, 2 * b + 1)
                        sp.dma_start(wv, w_down[l, e].rearrange("(k p) n -> p k n", p=P)).then_inc(d_loaded, 16)
                    with sp.If(l < DEPTH - 1):
                        sp.wait_ge(g_filled, n_blocks + 1)
                        sp.wait_ge(u_filled, n_blocks + 1)
                        sp.wait_ge(y_filled, 2 * n_blocks + 1)
                        load_ahead(sp, nc.s_assert_within(l + 1, 1, DEPTH - 1, skip_runtime_bounds_check_because="only before the last layer"))
                    with sp.If(l > DEPTH - 2):
                        for c in range(NC):
                            out = (y_prompt, y_sample)[SEQ_OF[c]]
                            sp.wait_ge(x_ready, 2 * NC + c + 1)
                            sp.dma_start(out[0].rearrange("(c p) d -> c p d", p=P)[c - BASE[SEQ_OF[c]]], x[:, c, :]).then_inc(out_stored, 16)

                @block.gpsimd
                def _(pool):
                    nc.gpsimd.memset(va[:, :, :, MD:MD + 1], 1.0).then_inc(ones_made, 1)
                    m = 0
                    for g, (h, s) in enumerate(ML_GROUPS):
                        for sc in range(CHUNKS[s]):
                            for d in range(2):
                                pool.wait_ge(d_exp, m + 1)
                                diag = dec[:, d, 0:P] if d == 0 else dec[:, d, sc * P:(sc + 1) * P]
                                sign = 1 if d == 0 else -1
                                nc.gpsimd.affine_select(out=diag, in_=diag, compare_op=ALU.is_ge, fill=0.0, base=0,
                                                        pattern=[[sign, P]], channel_multiplier=-sign).then_inc(d_masked, 1)
                                m += 1
                    pool.wait_ge(ids_ready, 1)
                    pool.wait_ge(zeros_stored, 64)
                    for a in range(2):
                        for c in range(NC):
                            nc.gpsimd.indirect_dma_start(
                                slots_x[:, :], bass.IndirectOffsetOnAxis(ap=slot_ids[:, a * NC + c:a * NC + c + 1].bitcast(U32), axis=0),
                                x[:, c, :], None).then_inc(scattered, 16)
                    n_blocks = pool.value_load(r_nbi[0:1, 0:1], min_val=1, max_val=BLOCKS)
                    pool.wait_ge(y_stored, 16 * n_blocks + 16)
                    pool.sem_inc(all_stored, 1)
                    pool.wait_ge(all_stored, 1)
                    for c in range(NC):
                        for a in range(2):
                            nc.gpsimd.indirect_dma_start(
                                gath[:, a, c, :], None, slots_y[:, :],
                                bass.IndirectOffsetOnAxis(ap=slot_ids[:, a * NC + c:a * NC + c + 1].bitcast(U32), axis=0)).then_inc(gathered[c], 16)

                @block.scalar
                def _(act):
                    steps = [0]

                    def step(ins):
                        steps[0] += 1
                        ins.then_inc(act_done, 1)
                        act.wait_ge(act_done, steps[0])

                    signals = {}

                    def own(sem_):
                        signals[sem_.name] = signals.get(sem_.name, 0) + 1
                        act.wait_ge(sem_, signals[sem_.name])

                    def rstd(out, var, n, scale, eps):
                        step(nc.scalar.activation(out, var, ACT.Ln, bias=eps, scale=scale))
                        return nc.scalar.activation(out, out, ACT.Exp, scale=-0.5)

                    def drain_copy(key, out, cols, parts=P):
                        tile_filled(act, key)
                        nc.scalar.activation(out, bank_of(key)[0:parts, 0:cols], ACT.Copy).then_inc(drain_sem(key), 1)
                        tile_drained(act, key)

                    act.preload_act_table_set("natural_log_exp_and_others")
                    for dst, src in ((gbias[:, :], gate_bias), (sink[:, :], attn_sink), (gmix[:, 0:ATT], attn_norm_g),
                                     (gmix[:, ATT:D], mlstm_norm_g)):
                        act.dma_start(dst, src[l].partition_broadcast(P)).then_inc(rows_loaded, 16)
                    act.dma_start(z[0:24, 0:P], conv_w[l].rearrange("t (j p) -> (t j) p", p=P)).then_inc(taps_loaded, 16)
                    act.dma_start(z[24:32, 0:P], conv_b[l].rearrange("(j p) -> j p", p=P)).then_inc(taps_loaded, 16)

                    for c in range(NC):
                        tile_filled(act, ("q", c))
                        nc.scalar.activation(y[:, c, 0:ATT].rearrange("p (j t d) -> p t j d", j=GRP, t=NKV),
                                             bank_of(("q", c))[:, :].rearrange("p (t j d) -> p t j d", j=GRP, t=NKV),
                                             ACT.Copy).then_inc(drain_sem(("q", c)), 1)
                        tile_drained(act, ("q", c))
                    drain_copy(("gi",), rows[:, 0, 0:512], 512, 8)
                    drain_copy(("gf",), rows[:, 1, 0:512], 512, 8)
                    tile_filled(act, ("gs",))
                    step(nc.scalar.activation(rows[:, 0, 512:T], bank_of(("gs",))[0:8, 0:256], ACT.Copy))
                    nc.scalar.activation(rows[:, 1, 512:T], bank_of(("gs",))[0:8, 256:512], ACT.Copy).then_inc(drain_sem(("gs",)), 1)
                    tile_drained(act, ("gs",))
                    tile_drained(act, ("gf",))
                    tile_drained(act, ("gs",))
                    step(nc.scalar.activation(rows[:, 2, :], rows[:, 1, :], ACT.Abs))
                    step(nc.scalar.activation(rows[:, 2, :], rows[:, 2, :], ACT.Exp, scale=-1.0))
                    nc.scalar.activation(rows[:, 2, :], rows[:, 2, :], ACT.Ln, bias=one[0:8, :]).then_inc(lf_part, 1)
                    own(lf_part)
                    for c in range(NC):
                        key = ("qt", c)
                        tile_filled(act, key)
                        nc.scalar.activation(qT[:, :, c * P:(c + 1) * P],
                                             bank_of(key)[:, :].rearrange("p (j t) -> p j t", j=GRP), ACT.Copy).then_inc(drain_sem(key), 1)
                        tile_drained(act, key)
                    act.wait_ge(z_ready, 1)
                    nc.scalar.activation(rows[:, 5, :], rows[:, 5, :], ACT.Exp, scale=-1.0).then_inc(z_ready, 1)
                    act.wait_ge(z_ready, 2)

                    def stream_tile(key):
                        if key[0] == "cv":
                            i = STREAM.index(key)
                            n = SEQS[key[2]]
                            lo = BASE[key[2]] * P
                            tile_drained(act, key)
                            if i:
                                act.wait_ge(cv_used, i)
                            nc.scalar.activation(esc[:, 0:n], conv[:, key[1], lo:lo + n], ACT.Exp, scale=-1.0).then_inc(cv_exp, 1)
                            own(cv_exp)
                        elif key[0] == "v":
                            tile_filled(act, key)
                            nc.scalar.activation(va[:, key[1], :, 0:MD], bank_of(key)[:, :].rearrange("p (h d) -> p h d", h=MH),
                                                 ACT.Copy).then_inc(drain_sem(key), 1)
                            tile_drained(act, key)
                        else:
                            tile_filled(act, key)
                            if key[1] == NC - 1:
                                act.wait_ge(zeros_stored, 64)
                            nc.scalar.activation(y[:, key[1], ATT:D], bank_of(key)[:, :], ACT.Exp, scale=-1.0).then_inc(drain_sem(key), 1)
                            tile_drained(act, key)

                    for i in range(13):
                        w = slot_tiles(i)
                        for half in range(2):
                            if i:
                                for j in (2 * half, 2 * half + 1):
                                    key = ("pt", i - 1, j)
                                    n = keys_of(GROUP_ORDER[i - 1][0])[1] * P
                                    tile_filled(act, key)
                                    nc.scalar.activation(ptb[:, j, 0:n], bank_of(key)[:, 0:n], ACT.Copy).then_inc(drain_sem(key), 1)
                                    tile_drained(act, key)
                            if half == 0 and w:
                                stream_tile(w[0])
                        if i < 12:
                            c, n = GROUP_ORDER[i]
                            nk = keys_of(c)[1] * P
                            act.wait_ge(m_ready, i + 1)
                            for j in range(GRP):
                                nc.scalar.activation(probs[:, j, 0:nk], probs[:, j, 0:nk], ACT.Exp, bias=st[:, 4 + j:5 + j],
                                                     accum_out=st[:, 8 + j:9 + j])
                            nc.scalar.activation(st[:, 12:16], st[:, 12:16], ACT.Exp).then_inc(p_ready, 1)
                            own(p_ready)
                        for t in w[1:]:
                            stream_tile(t)
                    tile_drained(act, ("pv", 11))
                    act.wait_ge(cv_used, 16)
                    for c in range(NC):
                        last = nc.scalar.activation(esc[:, :], y[:, c, 0:ATT], ACT.Square, accum_out=st[:, 20 + c:21 + c])
                        step(last)
                    rstd(st[:, 20:26], st[:, 20:26], 6, 1.0 / ATT, eps_rms).then_inc(att_rs, 1)
                    own(att_rs)
                    for c in range(NC):
                        key = ("yt", c, 0)
                        tile_filled(act, key)
                        nc.scalar.activation(xT[:, 0:4, c * P:(c + 1) * P],
                                             bank_of(key)[:, :].rearrange("p (k t) -> p k t", k=4), ACT.Copy).then_inc(drain_sem(key), 1)
                        tile_drained(act, key)

                    m, last_st = 0, None
                    for g in range(9):
                        if g < 8:
                            h, s = ML_GROUPS[g]
                            n = CHUNKS[s]
                            for d in range(2):
                                key = ("rb", g, d)
                                tile_filled(act, key)
                                nc.scalar.activation(rbc[:, d, 0:n * P], bank_of(key)[:, 0:n * P], ACT.Copy).then_inc(drain_sem(key), 1)
                                tile_drained(act, key)
                            tile_drained(act, ("rb", g, 0))
                            tile_drained(act, ("rb", g, 1))
                            for sc in range(n):
                                for d in range(2):
                                    if last_st and d == 0:
                                        act.wait_ge(sw_ready, m // 2)
                                    if last_st and d == 1:
                                        tile_drained(act, last_st)
                                    lo, hi = (sc, n) if d == 0 else (0, sc + 1)
                                    col = (BASE[s] + sc) * 8 + 4 * d + h
                                    nc.scalar.activation(dec[:, d, 0:(hi - lo) * P], rbc[:, d, lo * P:hi * P], ACT.Exp,
                                                         scale=-1.0, bias=zn[:, col:col + 1]).then_inc(d_exp, 1)
                                    own(d_exp)
                                    m += 1
                                last_st = ("st", g, sc)
                        if g:
                            gg = g - 1
                            h, s = ML_GROUPS[gg]
                            n = CHUNKS[s]
                            tile_drained(act, ("nm", gg, n - 1))
                            b = 30 + 4 * (gg % 2)
                            for t in range(n):
                                step(nc.scalar.activation(esc[:, 0:P], hsc[:, gg % 2, t, :], ACT.Square,
                                                          accum_out=st[:, b + t:b + t + 1]))
                            rstd(st[:, b:b + n], st[:, b:b + n], n, 1.0 / MD, eps_rms).then_inc(h_rs, 1)
                            own(h_rs)
                    for c in range(NC):
                        key = ("yt", c, 1)
                        tile_filled(act, key)
                        nc.scalar.activation(xT[:, 4:8, c * P:(c + 1) * P],
                                             bank_of(key)[:, :].rearrange("p (k t) -> p k t", k=4), ACT.Copy).then_inc(drain_sem(key), 1)
                        tile_drained(act, key)

                    def load_ln(i, g_, b_):
                        act.dma_start(lng, g_[l].partition_broadcast(P)).then_inc(ln_rows_loaded[i], 16)
                        act.dma_start(lnb, b_[l].partition_broadcast(P)).then_inc(ln_rows_loaded[i], 16)

                    def ln_scale(i):
                        act.wait_ge(ln_var, i + 1)
                        c = 40 + 2 * (i % 2)
                        rstd(st[:, c + 1:c + 2], st[:, c + 1:c + 2], 1, 1.0, eps_ln).then_inc(ln_rstd, 1)
                        own(ln_rstd)

                    act.wait_ge(y_ml, 8)
                    load_ln(0, ln1_g, ln1_b)
                    for c in range(NC):
                        ln_scale(c)
                    act.wait_ge(x_ready, NC)
                    load_ln(1, ln2_g, ln2_b)
                    for k in range(KD):
                        drain_copy(("mt", k), memT[:, k, :], 512)
                    for j in range(KD):
                        drain_copy(("km", j), km[:, j, :], 512)
                    for mm in range(2 * MC):
                        for h in range(2):
                            drain_copy(("vm", mm, h), vm[:, mm, 512 * h:512 * h + 512], 512)
                    for c in range(NC):
                        for h in range(2):
                            key = ("x2", c, h)
                            tile_filled(act, key)
                            nc.scalar.activation(xT[:, 4 * h:4 * h + 4, c * P:(c + 1) * P],
                                                 bank_of(key)[:, :].rearrange("p (k t) -> p k t", k=4), ACT.Copy).then_inc(drain_sem(key), 1)
                            tile_drained(act, key)
                    for j in range(KD):
                        for s in range(2):
                            lo = BASE[s] * P
                            drain_copy(("qx", j, s), qx[:, j, lo:lo + SEQS[s]], SEQS[s])
                    def cross_tail(cp):
                        for m in range(0, 4, 2):
                            key = ("ox", cp, m)
                            tile_filled(act, key)
                            nc.scalar.activation(xT[:, 2 * m:2 * m + 2, cp * 256:(cp + 1) * 256],
                                                 bank_of(key)[:, :].rearrange("p (k t) -> p k t", k=2), ACT.Copy).then_inc(drain_sem(key), 1)
                            tile_drained(act, key)
                        if cp:
                            ln_scale(xl + 2 * cp - 2)
                            ln_scale(xl + 2 * cp - 1)

                    xl = 6
                    for i in range(12):
                        act.wait_ge(xm_ready, i + 1)
                        key = ("sx", i)
                        if i >= 2:
                            tile_filled(act, ("px", i - 2))
                        for h in range(2):
                            o = 50 + 8 * (i % 2)
                            last = nc.scalar.activation(xp[:, i % 2, h * NMEM:(h + 1) * NMEM], bank_of(key)[:, h * NMEM:(h + 1) * NMEM],
                                                        ACT.Exp, scale=1.0 / 16.0, bias=st[:, o + h:o + h + 1],
                                                        accum_out=st[:, o + 2 + h:o + 3 + h])
                            if h == 0:
                                step(last)
                            else:
                                last.then_inc(drain_sem(key), 1)
                                tile_drained(act, key)
                        if i:
                            c, hp = X_ITEMS[i - 1]
                            key = ("px", i - 1)
                            tile_filled(act, key)
                            if (i - 1) % 4 == 0 and i > 1:
                                tile_filled(act, ("ox", (i - 1) // 4 - 1, 3))
                            nc.scalar.activation(xpt[:, 2 * hp:2 * hp + 2, :, (c % 2) * P:(c % 2 + 1) * P],
                                                 bank_of(key)[:, :].rearrange("p (h m t) -> p h m t", h=2, m=MC),
                                                 ACT.Copy).then_inc(drain_sem(key), 1)
                            tile_drained(act, key)
                        if i and (i - 1) % 4 == 3:
                            cross_tail((i - 1) // 4)
                    c, hp = X_ITEMS[11]
                    key = ("px", 11)
                    tile_filled(act, key)
                    nc.scalar.activation(xpt[:, 2 * hp:2 * hp + 2, :, P:2 * P],
                                         bank_of(key)[:, :].rearrange("p (h m t) -> p h m t", h=2, m=MC),
                                         ACT.Copy).then_inc(drain_sem(key), 1)
                    tile_drained(act, key)
                    cross_tail(2)
                    ln_scale(xl + 4)
                    ln_scale(xl + 5)
                    act.wait_ge(x_ready, 2 * NC)
                    load_ln(2, ln3_g, ln3_b)
                    for c in range(NC):
                        key = ("x3", c, 0)
                        tile_filled(act, key)
                        nc.scalar.activation(xT[:, 0:4, c * P:(c + 1) * P],
                                             bank_of(key)[:, :].rearrange("p (k t) -> p k t", k=4), ACT.Copy).then_inc(drain_sem(key), 1)
                        tile_drained(act, key)
                    tile_filled(act, ("rt",))
                    nc.scalar.activation(r_s, bank_of(("rt",))[:, 0:NS_], ACT.Exp, scale=-1.0).then_inc(drain_sem(("rt",)), 1)
                    act.wait_ge(ids_ready, 1)
                    n_blocks = act.value_load(r_nbi[0:1, 0:1], min_val=1, max_val=BLOCKS)
                    act.sem_inc(g_ready, 1)
                    act.sem_inc(yl_ready, 1)
                    act.sem_inc(y_stored, 16)

                    def block_xT():
                        nc.scalar.activation(xbT[:, 0:4, :], banks[0][:, :].rearrange("p (k t) -> p k t", k=4), ACT.Copy)
                        nc.scalar.activation(xbT[:, 4:8, :], banks[1][:, :].rearrange("p (k t) -> p k t", k=4),
                                             ACT.Copy).then_inc(xT_ready, 1)
                        own(xT_ready)

                    act.preload_act_table(ACT.Silu)
                    act.wait_ge(xT_filled, 2)
                    block_xT()
                    with act.Fori(0, n_blocks) as b:
                        act.wait_ge(h_done, b + 1)
                        act.wait_ge(g_filled, b + 2)
                        nc.scalar.activation(gact, banks[2][:, :], ACT.Silu).then_inc(g_ready, 1)
                        act.wait_ge(xT_filled, 2 * b + 4)
                        block_xT()
                        act.wait_ge(hT_filled, b + 1)
                        nc.scalar.activation(hbT, banks[4][:, :].rearrange("p (k t) -> p k t", k=4), ACT.Copy).then_inc(hT_ready, 1)
                        act.wait_ge(y_stored, 16 * b + 16)
                        act.wait_ge(y_filled, 2 * b + 2)
                        nc.scalar.activation(yb[:, 0:512], banks[5][:, :], ACT.Copy).then_inc(yl_ready, 1)
                        act.wait_ge(yl_ready, b + 2)
                        act.wait_ge(yr_ready, b + 2)
                        act.dma_start(slots_y.rearrange("(b p) d -> b p d", p=P)[b], yb).then_inc(y_stored, 16)
                    act.preload_act_table_set("natural_log_exp_and_others")
                    for c in range(NC + 1):
                        if c < NC:
                            ln_scale(12 + c)
                        if c:
                            key = ("xn", c - 1, 0)
                            tile_filled(act, key)
                            nc.scalar.activation(xT[:, 0:4, (c - 1) * P:c * P],
                                                 bank_of(key)[:, :].rearrange("p (k t) -> p k t", k=4), ACT.Copy).then_inc(drain_sem(key), 1)
                            tile_drained(act, key)

                @block.vector
                def _(dve):
                    steps = [0]

                    def step(ins):
                        steps[0] += 1
                        ins.then_inc(dve_done, 1)
                        dve.wait_ge(dve_done, steps[0])

                    signals = {}

                    def own(sem_):
                        signals[sem_.name] = signals.get(sem_.name, 0) + 1
                        dve.wait_ge(sem_, signals[sem_.name])

                    v = nc.vector

                    def drain_xT(key, c):
                        tile_filled(dve, key)
                        v.tensor_copy(xT[:, 4:8, c * P:(c + 1) * P],
                                      bank_of(key)[:, :].rearrange("p (k t) -> p k t", k=4)).then_inc(drain_sem(key), 1)
                        tile_drained(dve, key)

                    v.memset(rows[:, 7, :], 1.0)
                    dve.wait_ge(rows_loaded, 4 * 16)
                    for c in range(NC):
                        key = ("kvg", c)
                        tile_filled(dve, key)
                        v.tensor_copy(kv[:, c, :], bank_of(key)[:, 0:256])
                        v.tensor_tensor(gts[:, c * NG:(c + 1) * NG].rearrange("p (g d h) -> p d g h", g=2, d=2),
                                        bank_of(key)[:, 256:272].rearrange("p (d g h) -> p d g h", g=2, d=2),
                                        gbias[:, :].rearrange("p (d g h) -> p d g h", g=2, d=2), ALU.add).then_inc(drain_sem(key), 1)
                        tile_drained(dve, key)
                    tile_drained(dve, ("kvg", NC - 1))

                    def rope(view, heads):
                        n = NC * heads * HALF
                        shape = [P, NC, heads, HALF]
                        t = [z[:, 1024 + a * n:1024 + (a + 1) * n].rearrange("p (c h d) -> p c h d", c=NC, h=heads) for a in range(4)]
                        cos, sin = (cst[:, o:o + NC * HALF].rearrange("p (c d) -> p c d", c=NC).unsqueeze(2).broadcast_to(shape)
                                    for o in (C_COS, C_SIN))
                        x1, x2 = view[:, :, :, 0:HALF], view[:, :, :, HALF:ROT]
                        v.tensor_tensor(t[0], x1, cos, ALU.mult)
                        v.tensor_tensor(t[1], x2, sin, ALU.mult)
                        v.tensor_tensor(t[2], x2, cos, ALU.mult)
                        step(v.tensor_tensor(t[3], x1, sin, ALU.mult))
                        v.tensor_tensor(x1, t[0], t[1], ALU.subtract)
                        return v.tensor_tensor(x2, t[2], t[3], ALU.add)

                    k_heads = kv[:, :, 0:NKV * HD].rearrange("p c (h d) -> p c h d", h=NKV)
                    rope(k_heads, NKV).then_inc(k_roped, 1)
                    own(k_roped)
                    tile_drained(dve, ("q", NC - 1))
                    q_heads = y[:, :, 0:ATT].rearrange("p c (h d) -> p c h d", h=NH)
                    rope(q_heads, NH).then_inc(q_roped, 1)
                    own(q_roped)
                    for key, lo, n in ((("kt0",), 0, 512), (("kt1",), 512, 256)):
                        tile_filled(dve, key)
                        v.tensor_copy(kT[:, lo:lo + n], bank_of(key)[:, 0:n]).then_inc(drain_sem(key), 1)
                        tile_drained(dve, key)
                    tile_filled(dve, ("cw",))
                    v.tensor_copy(cwb[:, :], bank_of(("cw",))[:, 0:32]).then_inc(drain_sem(("cw",)), 1)
                    tile_drained(dve, ("cw",))

                    dve.wait_ge(lf_part, 1)
                    r = [rows[:, j, :] for j in range(8)]
                    fwd, bwd = cst[0:8, C_FWD:C_FWD + 1], cst[0:8, C_BWD:C_BWD + 1]
                    step(v.scalar_tensor_tensor(out=r[1], in0=r[1], scalar=0.0, in1=r[2], op0=ALU.min, op1=ALU.subtract))

                    def scans(src_a, src_b, op0, op1, out):
                        for lo, n in ((0, 512), (512, 256)):
                            w = slice(lo, lo + n)
                            v.tensor_tensor_scan(r[2][:, w], src_a[:, w], src_b[:, w], 0.0, op0, op1)
                            back = slice(lo + n - 1, lo - 1 if lo else None, -1)
                            step(v.tensor_tensor_scan(r[6][:, back], src_a[:, back], src_b[:, back], 0.0, op0, op1))
                        step(v.tensor_scalar(r[6], r[6], bwd, None, ALU.mult))
                        step(v.scalar_tensor_tensor(out=out, in0=r[2], scalar=fwd, in1=r[6], op0=ALU.mult, op1=ALU.add))

                    scans(r[7], r[1], ALU.mult, ALU.add, r[3])
                    step(v.tensor_tensor(r[4], r[0], r[3], ALU.subtract))
                    scans(r[4], r[4], ALU.max, ALU.max, rrow[0:8, :])
                    v.tensor_tensor(r[5], r[3], rrow[0:8, :], ALU.add).then_inc(z_ready, 1)
                    own(z_ready)
                    tile_filled(dve, ("zt",))
                    v.tensor_copy(zn[:, :], bank_of(("zt",))[:, 0:48])
                    v.tensor_copy(thr[:, :], bank_of(("zt",))[:, 48:96]).then_inc(drain_sem(("zt",)), 1)
                    tile_drained(dve, ("zt",))

                    def conv_finish(i):
                        _, j, s = STREAM[i]
                        n, lo = SEQS[s], BASE[s] * P
                        dve.wait_ge(cv_exp, i + 1)
                        step(v.tensor_scalar(esc[:, 0:n], esc[:, 0:n], 1.0, None, ALU.add))
                        step(v.reciprocal(esc[:, 0:n], esc[:, 0:n]))
                        c_ = conv[:, j, lo:lo + n]
                        v.scalar_tensor_tensor(out=c_, in0=c_, scalar=1.0 if j < 4 else float(MD) ** -0.5, in1=esc[:, 0:n],
                                               op0=ALU.mult, op1=ALU.mult).then_inc(cv_used, 1)
                        own(cv_used)

                    def stream_tile(key):
                        i = STREAM.index(key)
                        if key[0] == "cv":
                            _, j, s = key
                            n, lo = SEQS[s], BASE[s] * P
                            ps = bank_of(key)
                            c_ = conv[:, j, lo:lo + n]
                            tile_filled(dve, key)
                            tap = [cwb[:, t * 8 + j:t * 8 + j + 1] for t in range(4)]
                            step(v.tensor_scalar(c_, ps[:, 0:n], tap[1], tap[3], ALU.mult, ALU.add))
                            step(v.scalar_tensor_tensor(out=c_[:, 1:n], in0=ps[:, 0:n - 1], scalar=tap[0], in1=c_[:, 1:n],
                                                        op0=ALU.mult, op1=ALU.add))
                            v.scalar_tensor_tensor(out=c_[:, 0:n - 1], in0=ps[:, 1:n], scalar=tap[2], in1=c_[:, 0:n - 1],
                                                   op0=ALU.mult, op1=ALU.add).then_inc(drain_sem(key), 1)
                            tile_drained(dve, key)
                        if 1 <= i <= 16:
                            conv_finish(i - 1)
                        if key[0] == "o":
                            tile_drained(dve, key)
                            o_ = y[:, key[1], ATT:D]
                            step(v.tensor_scalar(o_, o_, 1.0, None, ALU.add))
                            step(v.reciprocal(o_, o_))
                            step(v.tensor_tensor(o_, o_, gmix[:, ATT:D], ALU.mult))

                    dve.wait_ge(taps_loaded, 32)
                    for i in range(13):
                        w = slot_tiles(i)
                        if i:
                            dve.wait_ge(p_ready, i)
                            ro = 110 + 4 * ((i - 1) % 2)
                            step(v.tensor_tensor(st[:, ro:ro + 4], st[:, 8:12], st[:, 12:16], ALU.add))
                            step(v.reciprocal(st[:, ro:ro + 4], st[:, ro:ro + 4]))
                        if w:
                            stream_tile(w[0])
                        if i < 12:
                            c, n = GROUP_ORDER[i]
                            _, nb, m0 = keys_of(c)
                            nk = nb * P
                            if i:
                                tile_filled(dve, ("pt", i - 1, 3))
                            else:
                                tile_filled(dve, ("cw",))
                            for j in range(GRP):
                                key = ("sc", i, j)
                                tile_filled(dve, key)
                                v.scalar_tensor_tensor(out=probs[:, j, 0:nk], in0=bank_of(key)[:, 0:nk], scalar=HD ** -0.5,
                                                       in1=cst[:, C_MASK + m0:C_MASK + m0 + nk], op0=ALU.mult,
                                                       op1=ALU.add).then_inc(drain_sem(key), 1)
                                tile_drained(dve, key)
                            for j in range(GRP):
                                tile_drained(dve, ("sc", i, j))
                            step(v.tensor_reduce(st[:, 0:4], probs[:, :, 0:nk], AX.X, ALU.max))
                            sk = sink[:, n * GRP:(n + 1) * GRP]
                            step(v.tensor_tensor(st[:, 0:4], st[:, 0:4], sk, ALU.max))
                            v.tensor_scalar(st[:, 4:8], st[:, 0:4], -1.0, None, ALU.mult)
                            v.tensor_tensor(st[:, 12:16], sk, st[:, 0:4], ALU.subtract).then_inc(m_ready, 1)
                            own(m_ready)
                        for t in w[1:]:
                            stream_tile(t)
                        if i:
                            c, n = GROUP_ORDER[i - 1]
                            key = ("pv", i - 1)
                            tile_filled(dve, key)
                            step_ = v.tensor_tensor(y[:, c, n * 256:(n + 1) * 256].rearrange("p (j d) -> p j d", j=GRP),
                                                    bank_of(key)[:, 0:256].rearrange("p (j d) -> p j d", j=GRP),
                                                    st[:, ro:ro + 4].unsqueeze(2).broadcast_to([P, GRP, HD]), ALU.mult)
                            step_.then_inc(drain_sem(key), 1)
                            tile_drained(dve, key)
                    dve.wait_ge(att_rs, 1)
                    for c in range(NC):
                        v.scalar_tensor_tensor(out=y[:, c, 0:ATT], in0=y[:, c, 0:ATT], scalar=st[:, 20 + c:21 + c],
                                               in1=gmix[:, 0:ATT], op0=ALU.mult, op1=ALU.mult).then_inc(y_att, 1)
                        own(y_att)

                    m = 0
                    for g in range(10):
                        if g < 8:
                            h, s = ML_GROUPS[g]
                            n = CHUNKS[s]
                            for sc in range(n):
                                key = ("st", g, sc)
                                tile_filled(dve, key)
                                for d in range(2):
                                    dve.wait_ge(d_masked, m + 1)
                                    lo, hi = (sc, n) if d == 0 else (0, sc + 1)
                                    ins = v.tensor_tensor(sw_at(g, d, n, sc, lo, hi), bank_of(key)[:, lo * P:hi * P],
                                                          dec[:, d, 0:(hi - lo) * P], ALU.mult)
                                    if d == 0:
                                        ins.then_inc(sw_ready, 1)
                                        own(sw_ready)
                                    else:
                                        ins.then_inc(drain_sem(key), 1)
                                        tile_drained(dve, key)
                                    m += 1
                        if 1 <= g < 9:
                            gg = g - 1
                            h, s = ML_GROUPS[gg]
                            for t in range(CHUNKS[s]):
                                key = ("nm", gg, t)
                                c = BASE[s] + t
                                tile_filled(dve, key)
                                ps = bank_of(key)[:, :].rearrange("p (d e) -> p d e", d=2)
                                floor = thr[:, c * 8:c * 8 + 8].rearrange("p (d h) -> p d h", d=2)[:, :, h:h + 1]
                                den = st[:, 100:102].rearrange("p (d e) -> p d e", d=2)
                                step(v.tensor_reduce(st[:, 100:102], ps[:, :, MD:MD + 1], AX.X, ALU.max, apply_absolute_value=True))
                                step(v.tensor_tensor(den, den, floor, ALU.max))
                                step(v.reciprocal(den, den))
                                hs = hsc[:, gg % 2, t, :]
                                step(v.tensor_scalar(hs, ps[:, 0, 0:MD], st[:, 100:101], None, ALU.mult))
                                v.scalar_tensor_tensor(out=hs, in0=ps[:, 1, 0:MD], scalar=st[:, 101:102], in1=hs,
                                                       op0=ALU.mult, op1=ALU.add).then_inc(drain_sem(key), 1)
                                tile_drained(dve, key)
                        if g >= 2:
                            gg = g - 2
                            h, s = ML_GROUPS[gg]
                            dve.wait_ge(h_rs, gg + 1)
                            b = 30 + 4 * (gg % 2)
                            for t in range(CHUNKS[s]):
                                o_ = y[:, BASE[s] + t, ATT + h * MD:ATT + (h + 1) * MD]
                                ins = v.scalar_tensor_tensor(out=o_, in0=hsc[:, gg % 2, t, :], scalar=st[:, b + t:b + t + 1],
                                                             in1=o_, op0=ALU.mult, op1=ALU.mult)
                            ins.then_inc(y_ml, 1)
                            own(y_ml)

                    def ln_stats(i, c):
                        o = 40 + 2 * (i % 2)
                        b = st[:, 70:82]
                        v.bn_stats(b[:, 0:6], x[:, c, 0:512])
                        step(v.bn_stats(b[:, 6:12], x[:, c, 512:D]))
                        v.bn_aggr(st[:, o:o + 2], b).then_inc(ln_var, 1)
                        own(ln_var)

                    def ln_apply(i, c):
                        o = 40 + 2 * (i % 2)
                        dve.wait_ge(ln_rows_loaded[i // NC], 32)
                        dve.wait_ge(ln_rstd, i + 1)
                        step(v.scalar_tensor_tensor(out=x[:, c, :], in0=x[:, c, :], scalar=st[:, o:o + 1], in1=lng,
                                                    op0=ALU.subtract, op1=ALU.mult))
                        v.scalar_tensor_tensor(out=x[:, c, :], in0=x[:, c, :], scalar=st[:, o + 1:o + 2], in1=lnb,
                                               op0=ALU.mult, op1=ALU.add).then_inc(x_ready, 1)
                        own(x_ready)

                    def residual_ln(i, c, name):
                        for h in range(2):
                            key = (name, c, h)
                            tile_filled(dve, key)
                            xh = x[:, c, 512 * h:512 * h + 512]
                            v.scalar_tensor_tensor(out=xh, in0=xh, scalar=ALPHA, in1=bank_of(key)[:, :],
                                                   op0=ALU.mult, op1=ALU.add).then_inc(drain_sem(key), 1)
                            tile_drained(dve, key)
                        tile_drained(dve, (name, c, 0))
                        tile_drained(dve, (name, c, 1))
                        ln_stats(i, c)
                        ln_apply(i, c)

                    for c in range(NC):
                        residual_ln(c, c, "wo")

                    def cross_max(i):
                        o = 50 + 8 * (i % 2)
                        key = ("sx", i)
                        tile_filled(dve, key)
                        step(v.tensor_reduce(st[:, o:o + 2], bank_of(key)[:, :].rearrange("p (h m) -> p h m", h=2), AX.X, ALU.max))
                        v.tensor_scalar(st[:, o:o + 2], st[:, o:o + 2], -float(XD) ** -0.5, None, ALU.mult).then_inc(xm_ready, 1)
                        own(xm_ready)

                    def cross_norm(i):
                        o = 50 + 8 * (i % 2)
                        tile_drained(dve, ("sx", i))
                        step(v.reciprocal(st[:, o + 4:o + 6], st[:, o + 2:o + 4]))
                        for h in range(2):
                            ph = xp[:, i % 2, h * NMEM:(h + 1) * NMEM]
                            ins = v.tensor_scalar(ph, ph, st[:, o + 4 + h:o + 5 + h], None, ALU.mult)
                        ins.then_inc(xp_ready, 1)
                        own(xp_ready)

                    cross_max(0)
                    for i in range(12):
                        if i + 1 < 12:
                            cross_max(i + 1)
                        cross_norm(i)
                        if i % 4 == 3:
                            cp = i // 4
                            for mm in (1, 3):
                                key = ("ox", cp, mm)
                                tile_filled(dve, key)
                                v.tensor_copy(xT[:, 2 * mm:2 * mm + 2, cp * 256:(cp + 1) * 256],
                                              bank_of(key)[:, :].rearrange("p (k t) -> p k t", k=2)).then_inc(drain_sem(key), 1)
                                tile_drained(dve, key)
                            if cp:
                                for c in (2 * cp - 2, 2 * cp - 1):
                                    residual_ln(NC + c, c, "wx")
                    for c in (4, 5):
                        residual_ln(NC + c, c, "wx")
                    for c in range(NC):
                        drain_xT(("x3", c, 1), c)

                    tile_drained(dve, ("rt",))
                    step(v.tensor_scalar(r_s, r_s, 1.0, None, ALU.add))
                    step(v.reciprocal(r_s, r_s))

                    def by_chunk(a):
                        return a.rearrange("p (c e) -> p c e", c=NC)

                    def to_chunks(a):
                        return a.unsqueeze(1).broadcast_to([P, NC, NE])

                    step(v.tensor_tensor(by_chunk(r_sel), by_chunk(r_s), to_chunks(rbias[:, :]), ALU.add))

                    def ranks(val, n, out):
                        b1, b2 = (a[:, 0:n * 16].rearrange("p (g i j) -> p g i j", i=4, j=4) for a in (r_beat, r_beat2))
                        four = [P, n, 4, 4]
                        vi = val.rearrange("p (g i) -> p g i", i=4).unsqueeze(3).broadcast_to(four)
                        vj = val.rearrange("p (g j) -> p g j", j=4).unsqueeze(2).broadcast_to(four)
                        tri = cst[:, C_TRI:C_TRI + 16].rearrange("p (i j) -> p i j", i=4).unsqueeze(1).broadcast_to(four)
                        v.tensor_tensor(b1, vj, vi, ALU.is_gt)
                        step(v.tensor_tensor(b2, vj, vi, ALU.is_equal))
                        step(v.tensor_tensor(b2, b2, tri, ALU.mult))
                        step(v.tensor_tensor(b1, b1, b2, ALU.add))
                        step(v.tensor_reduce(out, b1, AX.X, ALU.add))

                    ranks(r_sel, 24, r_rank)
                    step(v.tensor_scalar(r_m, r_rank, 1.5, None, ALU.is_lt))
                    step(v.tensor_tensor(r_t1, r_m, r_sel, ALU.mult))
                    step(v.tensor_reduce(r_gs, r_t1.rearrange("p (g i) -> p g i", i=4), AX.X, ALU.add))
                    ranks(r_gs, NC, r_gr)
                    step(v.tensor_scalar(r_gr, r_gr, 0.5, None, ALU.is_lt))
                    m_ = r_m.rearrange("p (g i) -> p g i", i=4)
                    v.tensor_tensor(m_, m_, r_gr.unsqueeze(2).broadcast_to([P, 24, 4]), ALU.mult).then_inc(mask_ready, 1)
                    own(mask_ready)
                    dve.wait_ge(mask_ready, 1)
                    step(v.tensor_tensor(r_w, r_s, r_m, ALU.mult))
                    step(v.tensor_reduce(r_sum, by_chunk(r_w), AX.X, ALU.add))
                    step(v.reciprocal(r_sum, r_sum))
                    step(v.tensor_tensor(by_chunk(r_w), by_chunk(r_w), r_sum.unsqueeze(2).broadcast_to([P, NC, NE]), ALU.mult))
                    key = ("rank",)
                    tile_filled(dve, key)
                    v.tensor_copy(r_slot, bank_of(key)[:, 0:NS_])
                    v.tensor_copy(r_tot, bank_of(key)[:, NS_:2 * NS_]).then_inc(drain_sem(key), 1)
                    tile_drained(dve, key)
                    step(v.memset(r_cnt, 0.0))
                    tile_drained(dve, key)
                    for c in range(NC):
                        sl = slice(c * NE, (c + 1) * NE)
                        step(v.tensor_tensor(r_slot[:, sl], r_slot[:, sl], r_cnt, ALU.add))
                        step(v.tensor_tensor(r_cnt, r_cnt, r_tot[:, sl], ALU.add))
                    cmp_ = r_cmp[:, 0:NE * NC].rearrange("p (e j) -> p e j", e=NE)
                    step(v.tensor_tensor(cmp_, r_cnt.unsqueeze(2).broadcast_to([P, NE, NC]),
                                         cst[:, C_STEP:C_STEP + NC].unsqueeze(1).broadcast_to([P, NE, NC]), ALU.is_gt))
                    step(v.tensor_reduce(r_nb, cmp_, AX.X, ALU.add))
                    step(v.tensor_tensor_scan(r_end, cst[:, C_ONES:C_ONES + NE], r_nb, 0.0, ALU.mult, ALU.add))
                    step(v.tensor_tensor(r_start, r_end, r_nb, ALU.subtract))
                    step(v.tensor_scalar(r_start, r_start, float(P), None, ALU.mult))
                    step(v.tensor_tensor(by_chunk(r_slot), by_chunk(r_slot), to_chunks(r_start), ALU.add))
                    sa, sb_ = r_slots[:, 0:NC], r_slots[:, NC:2 * NC]
                    step(v.tensor_tensor(r_t1, r_slot, r_m, ALU.mult))
                    step(v.tensor_reduce(sb_, by_chunk(r_t1), AX.X, ALU.max))
                    step(v.tensor_scalar(r_t1, r_slot, FAR, None, ALU.subtract))
                    step(v.tensor_tensor(r_t1, r_t1, r_m, ALU.mult))
                    step(v.tensor_scalar(r_t1, r_t1, FAR, None, ALU.add))
                    step(v.tensor_reduce(sa, by_chunk(r_t1), AX.X, ALU.min))
                    for a, s_ in ((0, sa), (1, sb_)):
                        step(v.tensor_tensor(by_chunk(r_t1), by_chunk(r_slot), s_.unsqueeze(2).broadcast_to([P, NC, NE]), ALU.is_equal))
                        step(v.tensor_tensor(r_t1, r_t1, r_w, ALU.mult))
                        step(v.tensor_reduce(gw[:, a * NC:(a + 1) * NC], by_chunk(r_t1), AX.X, ALU.add))
                    v.tensor_copy(slot_ids, r_slots)
                    cmp_ = r_cmp[:, :].rearrange("p (b e) -> p b e", e=NE)
                    shape = [P, XBLOCKS, NE]
                    step(v.tensor_tensor(cmp_, cst[:, C_IOTA:C_IOTA + XBLOCKS].unsqueeze(2).broadcast_to(shape),
                                         r_end.unsqueeze(1).broadcast_to(shape), ALU.is_ge))
                    step(v.tensor_reduce(r_be, cmp_, AX.X, ALU.add))
                    v.tensor_scalar(r_bei, r_be, float(NE - 1), None, ALU.min)
                    v.tensor_copy(r_nbi, r_end[:, NE - 1:NE]).then_inc(ids_ready, 1)
                    own(ids_ready)
                    dve.wait_ge(scattered, l * (16 * 2 * NC) + 16 * 2 * NC)
                    for c in range(NC):
                        step(v.tensor_scalar(x[:, c, :], x[:, c, :], ALPHA, None, ALU.mult))
                    dve.wait_ge(ids_ready, 1)
                    n_blocks = dve.value_load(r_nbi[0:1, 0:1], min_val=1, max_val=BLOCKS)
                    dve.sem_inc(h_done, 1)
                    dve.sem_inc(yr_ready, 1)
                    with dve.Fori(0, n_blocks) as b:
                        dve.wait_ge(g_ready, b + 2)
                        dve.wait_ge(u_filled, b + 2)
                        v.tensor_tensor(hb, gact, banks[3][:, :], ALU.mult).then_inc(h_done, 1)
                        dve.wait_ge(y_stored, 16 * b + 16)
                        dve.wait_ge(y_filled, 2 * b + 3)
                        v.tensor_copy(yb[:, 512:D], banks[6][:, :]).then_inc(yr_ready, 1)
                    for c in range(NC + 1):
                        if c < NC:
                            dve.wait_ge(gathered[c], l * 32 + 32)
                            xc = x[:, c, :]
                            for a in range(2):
                                step(v.scalar_tensor_tensor(out=xc, in0=gath[:, a, c, :], scalar=gw[:, a * NC + c:a * NC + c + 1],
                                                            in1=xc, op0=ALU.mult, op1=ALU.add))
                            ln_stats(2 * NC + c, c)
                            ln_apply(2 * NC + c, c)
                        if c:
                            drain_xT(("xn", c - 1, 1), c - 1)

                @block.tensor
                def _(pe):
                    def take(key):
                        b, use = TILES[key]
                        if use:
                            pe.wait_ge(drained[b], use)
                        return banks[b]

                    def done(ins, key):
                        ins.then_inc(filled[TILES[key][0]], 1)

                    def unit_ready(name):
                        n = UNIT[name]
                        if n < AHEAD:
                            pe.wait_ge(ahead[n], l * 32 + 32)
                        else:
                            pe.wait_ge(unit_loaded[n % SLOTS], 32 * (n // SLOTS))

                    def turn4(key, source):
                        ps = take(key)
                        for k in range(4):
                            ins = pe.transpose(ps[:, k * P:(k + 1) * P], source(k), ident)
                        done(ins, key)

                    def product(key, n, lhs, rhs, ks=KD):
                        ps = take(key)
                        for k in range(ks):
                            ins = pe.matmul(ps[:, 0:n], lhs(k), rhs(k), start=(k == 0), stop=(k == ks - 1))
                        done(ins, key)

                    unit_ready("kvg")
                    wv = unit_view("kvg", 272)
                    for c in range(NC):
                        product(("kvg", c), 272, lambda k: xT[:, k, c * P:(c + 1) * P], lambda k: wv[:, k, :])
                    unit_ready("q")
                    wv = unit_view("q", 512)
                    for c in range(NC):
                        product(("q", c), 512, lambda k: xT[:, k, c * P:(c + 1) * P], lambda k: wv[:, k, :])
                    tile_drained(pe, ("kvg", NC - 1))

                    def gate_cols(c, g):
                        return gts[:, c * NG + 8 * g:c * NG + 8 * g + 8]

                    for name, g in (("gi", 0), ("gf", 1)):
                        ps = take((name,))
                        for c in range(4):
                            ins = pe.transpose(ps[0:8, c * P:(c + 1) * P], gate_cols(c, g), ident)
                        done(ins, (name,))
                    ps = take(("gs",))
                    for g in range(2):
                        for c in (4, 5):
                            o = g * 256 + (c - 4) * P
                            ins = pe.transpose(ps[0:8, o:o + P], gate_cols(c, g), ident)
                    done(ins, ("gs",))
                    pe.wait_ge(k_roped, 1)
                    for name, cs in (("kt0", range(0, 4)), ("kt1", range(4, 6))):
                        ps = take((name,))
                        for c in cs:
                            o = (c - cs[0]) * P
                            ins = pe.transpose(ps[:, o:o + P], kv[:, c, 0:P], ident)
                        done(ins, (name,))
                    pe.wait_ge(q_roped, 1)
                    for c in range(NC):
                        turn4(("qt", c), lambda k: y[:, c, k * P:(k + 1) * P])
                    pe.wait_ge(taps_loaded, 32)
                    ps = take(("cw",))
                    done(pe.transpose(ps[:, 0:32], z[0:32, 0:P], ident[0:32, 0:32]), ("cw",))
                    pe.wait_ge(z_ready, 2)
                    ps = take(("zt",))
                    for a, row in ((0, 4), (1, 5)):
                        for c in range(NC):
                            o = a * 48 + c * 8
                            ins = pe.transpose(ps[:, o:o + 8], rows[:, row, c * P:(c + 1) * P], ident[0:8, 0:8])
                    done(ins, ("zt",))

                    def stream_tile(key):
                        if key[0] == "cv":
                            _, j, s = key
                            name = "mq" if j < 4 else "mk"
                            unit_ready(name)
                            w = unit_view(name, 512)
                            jj, lo = j % 4, BASE[s] * P
                            product(key, SEQS[s], lambda k: w[:, k, jj * P:(jj + 1) * P], lambda k: xT[:, k, lo:lo + SEQS[s]])
                        else:
                            name = "mv" if key[0] == "v" else "mo"
                            unit_ready(name)
                            w = unit_view(name, 512)
                            c = key[1]
                            product(key, 512, lambda k: xT[:, k, c * P:(c + 1) * P], lambda k: w[:, k, :])

                    tile_drained(pe, ("qt", NC - 1))
                    tile_drained(pe, ("kt1",))
                    for i in range(13):
                        w = slot_tiles(i)

                        def turn_probs(j):
                            c, _ = GROUP_ORDER[i - 1]
                            nb = keys_of(c)[1]
                            key = ("pt", i - 1, j)
                            ps = take(key)
                            for k in range(nb):
                                ins = pe.transpose(ps[:, k * P:(k + 1) * P], probs[:, j, k * P:(k + 1) * P], ident)
                            done(ins, key)

                        if i:
                            pe.wait_ge(p_ready, i)
                            turn_probs(0)
                            turn_probs(1)
                        if w:
                            stream_tile(w[0])
                        if i:
                            turn_probs(2)
                            turn_probs(3)
                        if i < 12:
                            c, n = GROUP_ORDER[i]
                            k0, nb, _ = keys_of(c)
                            hp = slice(n * HD, (n + 1) * HD)
                            for j in range(GRP):
                                key = ("sc", i, j)
                                ps = take(key)
                                done(pe.matmul(ps[:, 0:nb * P], qT[hp, j, c * P:(c + 1) * P], kT[hp, k0 * P:(k0 + nb) * P],
                                               start=True, stop=True), key)
                        for t in w[1:]:
                            stream_tile(t)
                        if i:
                            c, n = GROUP_ORDER[i - 1]
                            k0, nb, _ = keys_of(c)
                            tile_drained(pe, ("pt", i - 1, 2))
                            tile_drained(pe, ("pt", i - 1, 3))
                            key = ("pv", i - 1)
                            ps = take(key)
                            for j in range(GRP):
                                for k in range(nb):
                                    ins = pe.matmul(ps[:, j * HD:(j + 1) * HD], ptb[:, j, k * P:(k + 1) * P],
                                                    kv[:, k0 + k, NKV * HD + n * HD:NKV * HD + (n + 1) * HD],
                                                    start=(k == 0), stop=(k == nb - 1))
                            done(ins, key)
                    for c in range(NC):
                        pe.wait_ge(y_att, c + 1)
                        turn4(("yt", c, 0), lambda k: y[:, c, k * P:(k + 1) * P])

                    pe.wait_ge(ones_made, 1)
                    pe.wait_ge(cv_used, 16)
                    tile_drained(pe, ("v", NC - 2))
                    tile_drained(pe, ("v", NC - 1))
                    for g in range(9):
                        if g < 8:
                            h, s = ML_GROUPS[g]
                            n, lo = CHUNKS[s], BASE[s] * P
                            for d in range(2):
                                key = ("rb", g, d)
                                ps = take(key)
                                done(pe.matmul(ps[:, 0:n * P], sel_rows(4 * d + h), rrow[0:8, lo:lo + n * P], start=True, stop=True), key)
                            for sc in range(n):
                                key = ("st", g, sc)
                                ps = take(key)
                                done(pe.matmul(ps[:, 0:n * P], conv[:, 4 + h, lo + sc * P:lo + (sc + 1) * P],
                                               conv[:, h, lo:lo + n * P], start=True, stop=True), key)
                        if g:
                            gg = g - 1
                            h, s = ML_GROUPS[gg]
                            n = CHUNKS[s]
                            tile_drained(pe, ("st", gg, n - 1))
                            for t in range(n):
                                key = ("nm", gg, t)
                                ps = take(key)
                                for d in range(2):
                                    ss = range(0, t + 1) if d == 0 else range(t, n)
                                    for sc in ss:
                                        ins = pe.matmul(ps[:, 256 * d:256 * d + MD + 1], sw_at(gg, d, n, sc, t, t + 1),
                                                        va[:, BASE[s] + sc, h, :], start=(sc == ss[0]), stop=(sc == ss[-1]))
                                done(ins, key)
                    for c in range(NC):
                        pe.wait_ge(y_ml, 7 if SEQ_OF[c] == 0 else 8)
                        turn4(("yt", c, 1), lambda k: y[:, c, ATT + k * P:ATT + (k + 1) * P])
                    unit_ready("wo0")
                    unit_ready("wo1")
                    wv2 = [unit_view("wo0", 512), unit_view("wo1", 512)]
                    for c in range(NC):
                        tile_drained(pe, ("yt", c, 1))
                        if c == 0:
                            tile_drained(pe, ("yt", NC - 1, 0))
                        for h in range(2):
                            product(("wo", c, h), 512, lambda k: xT[:, k, c * P:(c + 1) * P], lambda k: wv2[h][:, k, :])
                    unit_ready("mem")
                    s_ = UNIT["mem"] % SLOTS
                    mem = ring[:, s_ * 4096:(s_ + 1) * 4096].rearrange("p (m d) -> p m d", m=2 * MC)
                    for k in range(KD):
                        turn4(("mt", k), lambda m: mem[:, m, k * P:(k + 1) * P])
                    tile_drained(pe, ("mt", KD - 1))
                    for j in range(KD):
                        name = "wk0" if j < 4 else "wk1"
                        unit_ready(name)
                        w = unit_view(name, 512)
                        product(("km", j), 512, lambda k: w[:, k, (j % 4) * P:(j % 4 + 1) * P], lambda k: memT[:, k, :])
                    unit_ready("wv0")
                    unit_ready("wv1")
                    wv2 = [unit_view("wv0", 512), unit_view("wv1", 512)]
                    for m in range(2 * MC):
                        for h in range(2):
                            product(("vm", m, h), 512, lambda k: memT[:, k, m * P:(m + 1) * P], lambda k: wv2[h][:, k, :])
                    for c in range(NC):
                        pe.wait_ge(x_ready, c + 1)
                        for h in range(2):
                            turn4(("x2", c, h), lambda k: x[:, c, (4 * h + k) * P:(4 * h + k + 1) * P])
                    tile_drained(pe, ("x2", NC - 1, 0))
                    tile_drained(pe, ("x2", NC - 1, 1))
                    for j in range(KD):
                        name = "wq0" if j < 4 else "wq1"
                        unit_ready(name)
                        w = unit_view(name, 512)
                        for s in range(2):
                            lo = BASE[s] * P
                            product(("qx", j, s), SEQS[s], lambda k: w[:, k, (j % 4) * P:(j % 4 + 1) * P],
                                    lambda k: xT[:, k, lo:lo + SEQS[s]])
                    tile_drained(pe, ("qx", KD - 1, 0))
                    tile_drained(pe, ("qx", KD - 1, 1))

                    def cross_scores(i):
                        c, hp = X_ITEMS[i]
                        key = ("sx", i)
                        ps = take(key)
                        mo = SEQ_OF[c] * NMEM
                        for h in range(2):
                            for k in range(2):
                                j = 2 * (2 * hp + h) + k
                                ins = pe.matmul(ps[:, h * NMEM:(h + 1) * NMEM], qx[:, j, c * P:(c + 1) * P],
                                                km[:, j, mo:mo + NMEM], start=(k == 0), stop=(k == 1))
                        done(ins, key)

                    def cross_out(c):
                        if c == 0:
                            unit_ready("wx0")
                            unit_ready("wx1")
                        w2 = [unit_view("wx0", 512), unit_view("wx1", 512)]
                        for h in range(2):
                            product(("wx", c, h), 512, lambda k: xT[:, k, c * P:(c + 1) * P], lambda k: w2[h][:, k, :])

                    cross_scores(0)
                    for i in range(12):
                        if i + 1 < 12:
                            cross_scores(i + 1)
                        pe.wait_ge(xp_ready, i + 1)
                        turn4(("px", i), lambda q: xp[:, i % 2, q * P:(q + 1) * P])
                        if i % 4 == 3:
                            cp = i // 4
                            tile_drained(pe, ("px", i - 1))
                            tile_drained(pe, ("px", i))
                            for m in range(4):
                                key = ("ox", cp, m)
                                ps = take(key)
                                for jj in range(2):
                                    j = 2 * m + jj
                                    for k in range(MC):
                                        ins = pe.matmul(ps[:, jj * 256:(jj + 1) * 256],
                                                        vm[:, SEQ_OF[2 * cp] * MC + k, j * P:(j + 1) * P],
                                                        xpt[:, j // 2, k, :], start=(k == 0), stop=(k == MC - 1))
                                done(ins, key)
                            if cp:
                                for m in range(4):
                                    tile_drained(pe, ("ox", cp - 1, m))
                                cross_out(2 * cp - 2)
                                cross_out(2 * cp - 1)
                    for m in range(4):
                        tile_drained(pe, ("ox", 2, m))
                    cross_out(4)
                    cross_out(5)
                    for c in range(NC):
                        pe.wait_ge(x_ready, NC + c + 1)
                        for h in range(2):
                            turn4(("x3", c, h), lambda k: x[:, c, (4 * h + k) * P:(4 * h + k + 1) * P])
                    tile_drained(pe, ("x3", NC - 1, 0))
                    tile_drained(pe, ("x3", NC - 1, 1))
                    pe.wait_ge(router_loaded, 32)
                    ps = take(("rt",))
                    rw = rw_t[:, :].rearrange("p (k e) -> p k e", k=KD)
                    for c in range(NC):
                        for k in range(KD):
                            ins = pe.matmul(ps[:, c * NE:(c + 1) * NE], xT[:, k, c * P:(c + 1) * P], rw[:, k, :],
                                            start=(k == 0), stop=(k == KD - 1))
                    done(ins, ("rt",))
                    pe.wait_ge(mask_ready, 1)
                    ps = take(("rank",))
                    pe.matmul(ps[:, 0:NS_], cst[:, C_STRICT:C_STRICT + P], r_m, start=True, stop=True)
                    done(pe.matmul(ps[:, NS_:2 * NS_], cst[:, C_ONES:C_ONES + P], r_m, start=True, stop=True), ("rank",))

                    pe.wait_ge(ids_ready, 1)
                    n_blocks = pe.value_load(r_nbi[0:1, 0:1], min_val=1, max_val=BLOCKS)
                    pe.sem_inc(g_filled, 1)
                    pe.sem_inc(u_filled, 1)
                    pe.sem_inc(y_filled, 1)
                    for bk in range(7):
                        pe.wait_ge(drained[bk], USES_BEFORE_EXPERTS[bk])

                    def turn_block():
                        for h in range(2):
                            for k in range(4):
                                q = 4 * h + k
                                ins = pe.transpose(banks[h][:, k * P:(k + 1) * P], xb[:, q * P:(q + 1) * P], ident)
                            ins.then_inc(xT_filled, 1)

                    wg = ring[:, 2 * 4096:3 * 4096].rearrange("p (k n) -> p k n", k=KD)
                    wu = ring[:, 0:4096].rearrange("p (k n) -> p k n", k=KD)
                    wd = ring[:, 4096:2 * 4096].rearrange("p (k n) -> p k n", k=4)
                    pe.wait_ge(x_loaded, 16)
                    turn_block()
                    with pe.Fori(0, n_blocks) as b:
                        pe.wait_ge(xT_ready, b + 1)
                        pe.wait_ge(g_loaded, 16 * b + 16)
                        pe.wait_ge(g_ready, b + 1)
                        for k in range(KD):
                            ins = pe.matmul(banks[2][:, :], xbT[:, k, :], wg[:, k, :], start=(k == 0), stop=(k == KD - 1))
                        ins.then_inc(g_filled, 1)
                        pe.wait_ge(u_loaded, 16 * b + 16)
                        pe.wait_ge(h_done, b + 1)
                        for k in range(KD):
                            ins = pe.matmul(banks[3][:, :], xbT[:, k, :], wu[:, k, :], start=(k == 0), stop=(k == KD - 1))
                        ins.then_inc(u_filled, 1)
                        pe.wait_ge(x_loaded, 16 * b + 32)
                        turn_block()
                        pe.wait_ge(h_done, b + 2)
                        for k in range(4):
                            ins = pe.transpose(banks[4][:, k * P:(k + 1) * P], hb[:, k * P:(k + 1) * P], ident)
                        ins.then_inc(hT_filled, 1)
                        pe.wait_ge(hT_ready, b + 1)
                        pe.wait_ge(d_loaded, 16 * b + 16)
                        pe.wait_ge(yl_ready, b + 1)
                        pe.wait_ge(yr_ready, b + 1)
                        for h in range(2):
                            for k in range(4):
                                ins = pe.matmul(banks[5 + h][:, :], hbT[:, k, :], wd[:, k, 512 * h:512 * h + 512],
                                                start=(k == 0), stop=(k == 3))
                            ins.then_inc(y_filled, 1)
                    for c in range(NC):
                        pe.wait_ge(x_ready, 2 * NC + c + 1)
                        for h in range(2):
                            turn4(("xn", c, h), lambda k: x[:, c, (4 * h + k) * P:(4 * h + k + 1) * P])

            for s in layer_sems:
                nc.sync.sem_clear(s)
            nc.all_engine_barrier()

        with nc.Block() as end:
            @end.sync
            def _(sp):
                sp.wait_ge(out_stored, 16 * NC)


_INS = ["x_prompt", "x_sample", "mem_prompt", "mem_sample", "w_in", "gate_bias", "conv_w", "conv_b", "attn_sink",
        "attn_norm_g", "mlstm_norm_g", "w_out", "ln1_g", "ln1_b", "wq_mem", "wkv_mem", "wo_mem", "ln2_g", "ln2_b",
        "router_w", "router_bias", "w_gate", "w_up", "w_down", "ln3_g", "ln3_b"]


def kernel(**inputs):
    import concourse.bacc as _bacc
    from concourse.bass_utils import run_bass_kernel_spmd as _run

    nc = _bacc.Bacc("TRN2", target_bir_lowering=False, num_devices=1)
    arrays, args = {}, []
    for name in _INS:
        a = np.ascontiguousarray(inputs[name])
        arrays[f"in_{name}"] = a
        args.append(nc.dram_tensor(f"in_{name}", a.shape, mybir.dt.from_np(a.dtype), kind="ExternalInput").ap())
    arrays["in_consts"] = constants()
    args.append(nc.dram_tensor("in_consts", [P, C_ALL], F32, kind="ExternalInput").ap())
    outs = [nc.dram_tensor(f"out_{i}", [1, n, D], F32, kind="ExternalOutput").ap() for i, n in enumerate(SEQS)]
    build_program(nc, *args, *outs)
    r = _run(nc, [arrays], core_ids=[0])
    return tuple(r.results[0][f"out_{i}"] for i in range(2))
```

```python
from contextlib import ExitStack

import numpy as np

import concourse.bass as bass
from concourse import mybir

F32 = mybir.dt.float32
F32R = mybir.dt.float32r
I32 = mybir.dt.int32
U32 = mybir.dt.uint32
ALU = mybir.AluOpType
ACT = mybir.ActivationFunctionType
AX = mybir.AxisListType

P = 128
DEPTH = 2
D = 1024
KD = D // P
SEQS = (512, 256)
T = sum(SEQS)
NC = T // P
CHUNKS = tuple(n // P for n in SEQS)
BASE = (0, CHUNKS[0])
SEQ_OF = tuple(s for s in range(2) for _ in range(CHUNKS[s]))
HD = 64
NH = 8
NKV = 2
GRP = NH // NKV
ATT = NH * HD
MH = 4
MD = 128
ML = MH * MD
ROT = HD // 4
HALF = ROT // 2
IN_W = 2832
OFF_K, OFF_MQ, OFF_MK, OFF_MV, OFF_MO, OFF_G = 512, 768, 1280, 1792, 2304, 2816
NG = 16
NMEM = 256
MC = NMEM // P
XH = 4
XD = D // XH
NE = 16
GROUPS = 4
EPG = NE // GROUPS
FF = 512
BLOCKS = (2 * T - NE) // P + NE
XBLOCKS = BLOCKS + 1
ALPHA = (2.0 * DEPTH) ** 0.25
NEG = -1e30
SLOTS = 3
FAR = 1.0e6

C_ID, C_STRICT, C_ONES, C_MASK = 0, 128, 256, 384
C_TRI = 768
C_SEL = C_TRI + EPG * EPG
C_COS = C_SEL + 8 * P
C_SIN = C_COS + NC * HALF
C_FWD = C_SIN + NC * HALF
C_BWD, C_EPS_LN, C_EPS_RMS, C_ONE = C_FWD + 1, C_FWD + 2, C_FWD + 3, C_FWD + 4
C_STEP = C_FWD + 5
C_IOTA = C_STEP + NC
C_ALL = C_IOTA + XBLOCKS

M_QT, M_KT, M_KV, M_CONV = 0, 3072, 3840, 5376
M_V = M_CONV + 8 * T
M_ALL = M_V + NC * MH * (MD + 1)
SW_DIR = 1280
X_VM, X_MEMT = 0, M_CONV
X_KM = X_MEMT + KD * 2 * NMEM
X_P, X_PT = M_CONV, M_CONV + 1024
X_STATS = (50, 58, 84)
Z_S, Z_PT = 0, GRP * 384
Z_R, Z_H = 0, 1024
Z_ALL = 3080


def constants():
    c = np.zeros((P, C_ALL), np.float32)
    p = np.arange(P)
    c[:, C_ID:C_ID + P] = np.eye(P)
    c[:, C_STRICT:C_STRICT + P] = p[:, None] < p[None, :]
    c[:, C_ONES:C_ONES + P] = 1.0
    c[:, C_MASK:C_MASK + P] = np.where(p[None, :] >= p[:, None], 0.0, NEG)
    c[:, C_MASK + 2 * P:C_MASK + 3 * P] = np.where(p[None, :] <= p[:, None], 0.0, NEG)
    c[:, C_TRI:C_TRI + EPG * EPG] = [float(j < i) for i in range(EPG) for j in range(EPG)]
    for r in range(8):
        c[r, C_SEL + r * P:C_SEL + (r + 1) * P] = 1.0
    inv = np.float32(500000.0) ** (-np.arange(0, ROT, 2, dtype=np.float32) / np.float32(ROT))
    for ch in range(NC):
        pos = (p + P * (ch - BASE[SEQ_OF[ch]])).astype(np.float32)
        ang = pos[:, None] * inv[None, :].astype(np.float32)
        c[:, C_COS + ch * HALF:C_COS + (ch + 1) * HALF] = np.cos(ang)
        c[:, C_SIN + ch * HALF:C_SIN + (ch + 1) * HALF] = np.sin(ang)
    c[0:4, C_FWD] = 1.0
    c[4:8, C_BWD] = 1.0
    c[:, C_EPS_LN], c[:, C_EPS_RMS], c[:, C_ONE] = 1e-5, 1e-6, 1.0
    c[:, C_STEP:C_STEP + NC] = P * np.arange(NC)
    c[:, C_IOTA:C_IOTA + XBLOCKS] = np.arange(XBLOCKS)
    return c


GROUP_ORDER = [(c, n) for c in range(NC) for n in range(NKV)]
STREAM = ([("cv", 4 + j, s) for j in range(4) for s in range(2)] + [("cv", j, s) for j in range(4) for s in range(2)]
          + [("v", c) for c in range(NC)] + [("o", c) for c in range(NC)])
PER_SLOT = [3, 2, 2, 3, 2, 2, 3, 2, 2, 3, 2, 2]
STARTS = [sum(PER_SLOT[:i]) for i in range(13)]
ML_GROUPS = [(h, s) for h in range(MH) for s in range(2)]
X_ITEMS = [(c, hp) for c in range(NC) for hp in range(2)]


OUT_ORDER = ([("yt", c, 1) for c in range(4)] + [("wo", 0, 0), ("wo", 0, 1)] + [("yt", c, 1) for c in (4, 5)]
             + [("wo", c, h) for c in (1, 2) for h in range(2)] + [("mt", k) for k in range(KD)]
             + [("wo", c, h) for c in range(3, NC) for h in range(2)])
QUARTERS = [[("km", 2 * q), ("km", 2 * q + 1)] for q in range(4)] + [[("vm", q, 0), ("vm", q, 1)] for q in range(4)]
ROUTER_PARTS = ((0, 4), (4, 1), (5, 1))
ROUTER_ORDER = ([("wx", 4, 0), ("wx", 4, 1)] + [("x3", c, h) for c in (0, 1) for h in range(2)] + [("wx", 5, 0), ("wx", 5, 1)]
                + [("x3", c, h) for c in (2, 3) for h in range(2)] + [("rl", 0)]
                + [("x3", 4, 0), ("x3", 4, 1), ("rl", 1), ("x3", 5, 0), ("x3", 5, 1), ("rl", 2), ("rt",)])


def slot_tiles(i):
    return STREAM[STARTS[i]:STARTS[i + 1]] if 0 <= i < 12 else []


def keys_of(c):
    s = SEQ_OF[c]
    lo, hi = max(c - 1, BASE[s]), min(c + 1, BASE[s] + CHUNKS[s] - 1)
    return lo, hi - lo + 1, (lo - c + 1) * P


def tile_plan():
    place, used, turn = {}, [0] * 8, {}

    def add(key, banks):
        b = banks[turn.get(banks, 0) % len(banks)]
        turn[banks] = turn.get(banks, 0) + 1
        place[key] = (b, used[b])
        used[b] += 1

    every = tuple(range(8))
    for c in range(NC):
        add(("kvg", c), every)
    for c in range(NC):
        add(("q", c), every)
    for k in ("gi", "gf", "gs", "kt0", "kt1"):
        add((k,), every)
    for c in range(NC):
        add(("qt", c), every)
    add(("cw",), every)
    for i in range(13):
        w = slot_tiles(i)
        if i < 12:
            for j in range(GRP):
                add(("sc", i, j), (0, 1, 2, 3))
        if i:
            for j in range(GRP):
                add(("pt", i - 1, j), (4, 5))
        if w:
            add(w[0], (6, 7))
        if i == 0:
            add(("zt",), (4, 5))
        if i:
            add(("pv", i - 1), (4, 5))
        for t in w[1:]:
            add(t, (6, 7))
    for g in range(9):
        if g < 8:
            add(("rb", g, 0), (0, 1))
            add(("rb", g, 1), (0, 1))
            for s in range(CHUNKS[ML_GROUPS[g][1]]):
                add(("st", g, s), (2, 3, 4))
        if g == 0:
            for c in range(NC):
                add(("yt", c, 0), (5, 6, 7))
        if g:
            for t in range(CHUNKS[ML_GROUPS[g - 1][1]]):
                add(("nm", g - 1, t), (5, 6, 7))
    for key in OUT_ORDER:
        add(key, every)
    for keys in QUARTERS:
        for key in keys:
            add(key, every)
    for c in range(NC):
        for h in range(2):
            add(("x2", c, h), every)
    for j in range(KD):
        for s in range(2):
            add(("qx", j, s), every)
    add(("sx", 0), (0, 1, 2))
    add(("sx", 1), (0, 1, 2))
    for i in range(12):
        if i + 2 < 12:
            add(("sx", i + 2), (0, 1, 2))
        add(("px", i), (3, 4))
        if i % 4 == 3:
            for m in range(4):
                add(("ox", i // 4, m), (3, 4))
            if i // 4:
                for c in (2 * (i // 4) - 2, 2 * (i // 4) - 1):
                    for h in range(2):
                        add(("wx", c, h), (5, 6, 7))
    for key in ROUTER_ORDER:
        add(key, {"wx": (5, 6, 7), "x3": (0, 1, 2, 3), "rl": (4, 5, 6), "rt": (7,)}[key[0]])
    add(("rank",), (5,))
    before_experts = list(used)
    for c in range(NC):
        for h in range(2):
            add(("xn", c, h), every)
    return place, before_experts


TILES, USES_BEFORE_EXPERTS = tile_plan()

UNITS = [
    ("kvg", ("kvg", NC - 1)), ("q", ("q", NC - 1)), ("mk", ("cv", 7, 1)), ("mq", ("cv", 3, 1)),
    ("mv", ("v", NC - 1)), ("mo", ("o", NC - 1)), ("mem", ("mt", KD - 1)), ("wo0", ("wo", NC - 1, 1)),
    ("wo1", ("wo", NC - 1, 1)), ("wk0", ("km", 3)), ("wk1", ("km", KD - 1)), ("wv0", ("vm", 1, 1)),
    ("wv1", ("vm", 3, 1)), ("wq0", ("qx", 3, 1)), ("wq1", ("qx", KD - 1, 1)),
    ("wx0", ("wx", NC - 1, 1)), ("wx1", ("wx", NC - 1, 1)),
]
UNIT = {name: n for n, (name, _) in enumerate(UNITS)}
AHEAD = SLOTS
assert DEPTH == 2 and [name for name, _ in UNITS[:AHEAD]] == ["kvg", "q", "mk"]


def build_program(nc, x_prompt, x_sample, mem_prompt, mem_sample, w_in, gate_bias, conv_w, conv_b, attn_sink,
                  attn_norm_g, mlstm_norm_g, w_out, ln1_g, ln1_b, wq_mem, wkv_mem, wo_mem, ln2_g, ln2_b,
                  router_w, router_bias, w_gate, w_up, w_down, ln3_g, ln3_b, consts, y_prompt, y_sample,
                  stop_after=None):
    slots_x = nc.dram_tensor("slots_x", [XBLOCKS * P, D], F32).ap()
    slots_y = nc.dram_tensor("slots_y", [XBLOCKS * P, D], F32).ap()

    with ExitStack() as ctx:
        def sb(name, cols, dt=F32):
            return ctx.enter_context(nc.sbuf_tensor(name, [P, cols], dt))

        def sem(name):
            s = ctx.enter_context(nc.semaphore(name))
            return s

        layer_sems = []

        def lsem(name):
            s = sem(name)
            layer_sems.append(s)
            return s

        banks = [ctx.enter_context(nc.psum_tensor(f"bank{i}", [P, 512], F32)) for i in range(8)]

        def sb_both(name, cols):
            with nc.sbuf_tensor(name, [P, cols], F32) as plain:
                pass
            return plain, ctx.enter_context(nc.sbuf_tensor(name + "_parts", [P, cols], F32R))

        x_t = sb("x", NC * D)
        x = x_t[:, :].rearrange("p (c d) -> p c d", c=NC)
        xt_t, xt_parts = sb_both("x_transposed", KD * T)
        xT = xt_t[:, :].rearrange("p (k t) -> p k t", k=KD)
        ring = sb("weight_slots", SLOTS * 4096)
        y_t, y_parts = sb_both("mixed", NC * D)
        y = y_t[:, :].rearrange("p (c d) -> p c d", c=NC)
        qx = y_t[:, :].rearrange("p (k t) -> p k t", k=KD)
        mix, mix_parts = sb_both("mixer_region", M_ALL)
        z = sb("scratch", Z_ALL)
        rrow = sb("running_max_rows", T)
        cst = sb("constants", C_ALL)
        gmix = sb("mixer_norm_gains", D)
        esc = sb("silu_exp", 512)
        gts = sb("gates", NC * NG)
        gbias = sb("gate_bias_rows", NG)
        sink = sb("sink_rows", NH)
        rw_t = sb("router_weights", KD * NE)
        rbias = sb("router_bias_rows", NE)
        zn = sb("z_by_token", NC * 8)
        thr = sb("floor_by_token", NC * 8)
        cwb = sb("conv_taps", 32)
        st = sb("small", 120)

        ident = cst[:, C_ID:C_ID + P]
        eps_ln = cst[:, C_EPS_LN:C_EPS_LN + 1]
        eps_rms = cst[:, C_EPS_RMS:C_EPS_RMS + 1]
        one = cst[:, C_ONE:C_ONE + 1]

        def unit_view(name, cols, k=KD):
            s = UNIT[name] % SLOTS
            return ring[:, s * 4096:s * 4096 + k * cols].rearrange("p (k n) -> p k n", k=k)

        qT = mix[:, M_QT:M_QT + GRP * T].rearrange("p (j t) -> p j t", j=GRP)
        kT = mix[:, M_KT:M_KT + T]
        kv = mix[:, M_KV:M_KV + NC * 256].rearrange("p (c n) -> p c n", c=NC)
        conv = mix[:, M_CONV:M_CONV + 8 * T].rearrange("p (j t) -> p j t", j=8)
        va = mix[:, M_V:M_ALL].rearrange("p (c h d) -> p c h d", c=NC, h=MH)
        rows = mix[0:8, M_CONV:M_CONV + 8 * T].rearrange("p (j t) -> p j t", j=8)
        vm = mix[:, X_VM:X_VM + 4096].rearrange("p (m n) -> p m n", m=2 * MC)
        memT_hi = mix_parts[:, X_MEMT:X_MEMT + 4096].rearrange("p (k m) -> p k m", k=KD)
        memT_lo = y_parts[:, 0:4096].rearrange("p (k m) -> p k m", k=KD)

        def quarter_parts(q):
            if q in (0, 2):
                pair = mix_parts[:, 0:2048], mix_parts[:, 2048:4096]
            elif q % 2:
                pair = xt_parts[:, 0:2048], xt_parts[:, 2048:4096]
            else:
                pair = xt_parts[:, 4096:6144], y_parts[:, 4096:6144]
            return [a.rearrange("p (k n) -> p k n", k=KD) for a in pair]

        def quarter_unit(q):
            return ("wk0", "wk1", "wv0", "wv1")[q // 2]

        def quarter_raw(q):
            return unit_view(quarter_unit(q), 512)[:, :, 256 * (q % 2):256 * (q % 2) + 256]

        km = mix[:, X_KM:X_KM + 4096].rearrange("p (k m) -> p k m", k=KD)
        xp = mix[:, X_P:X_P + 1024].rearrange("p (b n) -> p b n", b=2)
        xpt = mix[:, X_PT:X_PT + 2048].rearrange("p (h m t) -> p h m t", h=XH, m=MC)
        probs = z[:, Z_S:Z_S + GRP * 384].rearrange("p (j n) -> p j n", j=GRP)
        ptb = z[:, Z_PT:Z_PT + GRP * 384].rearrange("p (j n) -> p j n", j=GRP)
        dec = xt_t[:, 4 * T:4 * T + 2048].rearrange("p (b d n) -> p b d n", b=2, d=2)
        rbc = z[:, Z_R:Z_R + 1024].rearrange("p (b n) -> p b n", b=2)
        hsc = z[:, Z_H:Z_H + 1024].rearrange("p (b c d) -> p b c d", b=2, c=4)
        lng = z[:, 0:D]
        lnb = z[:, D:2 * D]
        xb = xt_t[:, 0:1024]
        xbT = xt_t[:, 1024:2048].rearrange("p (k t) -> p k t", k=KD)
        gact = xt_t[:, 2048:2560]
        hb = xt_t[:, 2560:3072]
        hbT = xt_t[:, 3072:3584].rearrange("p (k t) -> p k t", k=4)
        yb = xt_t[:, 3584:4608]
        zero_rows = y[:, NC - 1, ATT:D]
        r_at = [0]

        def rt(n, dt=F32):
            a = y_t[:, r_at[0]:r_at[0] + n]
            r_at[0] += n
            return a if dt == F32 else a.bitcast(dt)

        NS_ = NC * NE
        r_s, r_sel, r_gs, r_m, r_w, r_t1, r_t2 = rt(NS_), rt(NS_), rt(24), rt(NS_), rt(NS_), rt(NS_), rt(NS_)
        r_beat, r_beat2 = rt(384), rt(384)
        r_rank, r_gr, r_sum = rt(NS_), rt(24), rt(NC)
        r_tot, r_cnt, r_nb, r_end, r_start, r_slot = rt(NS_), rt(NE), rt(NE), rt(NE), rt(NE), rt(NS_)
        r_cmp, r_be, r_bei = rt(XBLOCKS * NE), rt(XBLOCKS), rt(XBLOCKS, I32)
        r_nbi = rt(1, I32)
        r_slots, gw = rt(2 * NC), rt(2 * NC)
        slot_ids = rt(2 * NC, I32)
        gath = mix[:, 0:2 * NC * D].rearrange("p (a c d) -> p a c d", a=2, c=NC)

        scattered = sem("slots_scattered")
        gathered = [sem(f"outputs_gathered{c}") for c in range(NC)]
        consts_loaded = sem("constants_loaded")
        x_in = [sem(f"x_loaded{i}") for i in range(3)]
        router_loaded = sem("router_loaded")
        ahead = [sem(f"unit_loaded_ahead{n}") for n in range(AHEAD)]
        start_turned = sem("x_turned")
        start_left = sem("x_left_taken")
        start_right = sem("x_right_taken")
        zeros_made = sem("zeros_made")
        zeros_stored = sem("zeros_stored")
        out_stored = sem("out_stored")
        filled = [lsem(f"filled{b}") for b in range(8)]
        drained = [lsem(f"drained{b}") for b in range(8)]
        unit_loaded = [lsem(f"unit_loaded{s}") for s in range(SLOTS)]
        rows_loaded = lsem("layer_rows_loaded")
        taps_loaded = lsem("conv_taps_loaded")
        ln_rows_loaded = [lsem(f"ln_rows_loaded{i}") for i in range(3)]
        dve_done = lsem("dve_step_done")
        act_done = lsem("act_step_done")
        ones_made = lsem("value_ones_made")
        gates_ready = lsem("gates_ready")
        lf_part = lsem("log_forget_parts")
        z_ready = lsem("z_rows_ready")
        k_roped = lsem("k_roped")
        q_roped = lsem("q_roped")
        s_masked = lsem("scores_masked")
        m_ready = lsem("row_max_ready")
        p_ready = lsem("probs_ready")
        cv_exp = lsem("conv_exp_ready")
        cv_used = lsem("conv_exp_used")
        o_exp = lsem("o_exp_ready")
        att_rs = lsem("attention_rms_ready")
        y_att = lsem("attention_half_ready")
        d_exp = lsem("decay_ready")
        d_masked = lsem("decay_masked")
        sw_ready = lsem("weights_ready")
        h_rs = lsem("h_rms_ready")
        y_ml = lsem("mlstm_half_ready")
        ln_var = lsem("ln_variance_ready")
        ln_rstd = lsem("ln_rstd_ready")
        x_ready = lsem("x_ready")
        xm_ready = lsem("cross_max_ready")
        xe_ready = lsem("cross_exp_ready")
        xp_ready = lsem("cross_probs_ready")
        mask_ready = lsem("expert_mask_ready")
        slots_ready = lsem("slots_ready")
        ids_ready = lsem("block_experts_ready")
        x_loaded = lsem("block_x_loaded")
        g_loaded = lsem("gate_weights_loaded")
        u_loaded = lsem("up_weights_loaded")
        d_loaded = lsem("down_weights_loaded")
        xT_filled = lsem("block_xT_filled")
        xT_ready = lsem("block_xT_ready")
        g_filled = lsem("block_gate_filled")
        g_ready = lsem("block_silu_ready")
        u_filled = lsem("block_up_filled")
        ul_filled = lsem("block_up_left_filled")
        hl_done = lsem("block_h_left_ready")
        h_done = lsem("block_h_ready")
        hTl_filled = lsem("block_hT_left_filled")
        hTl_ready = lsem("block_hT_left_ready")
        hT_filled = lsem("block_hT_filled")
        hT_ready = lsem("block_hT_ready")
        y_filled = lsem("block_y_filled")
        yl_ready = lsem("block_y_left_ready")
        yr_ready = lsem("block_y_right_ready")
        y_stored = lsem("block_y_stored")
        all_stored = lsem("all_blocks_stored")
        mem_hi = lsem("memory_high_part_ready")
        w_hi = lsem("weights_high_part_ready")
        w_lo = lsem("weights_low_part_ready")
        ln_gained = lsem("layer_output_times_gain")
        ln_scaled = lsem("layer_output_scaled")
        x_out = lsem("layer_output_ready")

        def tile_filled(eng, key):
            b, use = TILES[key]
            eng.wait_ge(filled[b], use + 1)

        def tile_drained(eng, key):
            b, use = TILES[key]
            eng.wait_ge(drained[b], use + 1)

        def bank_of(key):
            return banks[TILES[key][0]]

        def drain_sem(key):
            return drained[TILES[key][0]]

        def sw_at(g, d, n, sc, lo, hi):
            if d == 0:
                o = sum(n - q for q in range(sc)) + lo - sc
            else:
                o = sum(q + 1 for q in range(sc)) + lo
            o = (g % 2) * 2 * SW_DIR + d * SW_DIR + o * P
            return mix[:, o:o + (hi - lo) * P]

        def sel_rows(r):
            return cst[0:8, C_SEL + r * P:C_SEL + (r + 1) * P]

        def load_ahead(sp, layer):
            src = w_in[layer].rearrange("(k p) n -> p k n", p=P)
            v = unit_view("kvg", 272)
            sp.dma_start(v[:, :, 0:256], src[:, :, OFF_K:OFF_K + 256]).then_inc(ahead[0], 16)
            sp.dma_start(v[:, :, 256:272], src[:, :, OFF_G:OFF_G + NG]).then_inc(ahead[0], 16)
            for n, off in ((1, 0), (2, OFF_MK)):
                v = unit_view(UNITS[n][0], 512)
                for h in range(2):
                    sp.dma_start(v[:, 4 * h:4 * h + 4, :], src[:, 4 * h:4 * h + 4, off:off + 512]).then_inc(ahead[n], 16)

        X_PARTS = ((0, 2), (2, 2), (4, 2))
        with nc.Block() as start:
            @start.sync
            def _(sp):
                sp.dma_start(cst[:, :], consts).then_inc(consts_loaded, 16)
                xp_src = x_prompt[0].rearrange("(c p) d -> p c d", p=P)
                for i, src in enumerate((xp_src[:, 0:2, :], xp_src[:, 2:4, :], x_sample[0].rearrange("(c p) d -> p c d", p=P))):
                    sp.dma_start(x[:, 2 * i:2 * i + 2, :], src).then_inc(x_in[i], 16)
                load_ahead(sp, 0)
                sp.dma_start(rw_t[:, :].rearrange("p (k e) -> p k e", k=KD),
                             router_w.rearrange("(k p) e -> p k e", p=P)).then_inc(router_loaded, 16)
                sp.dma_start(rbias[:, :], router_bias.partition_broadcast(P)).then_inc(router_loaded, 16)

            @start.gpsimd
            def _(pool):
                nc.gpsimd.memset(zero_rows, 0.0).then_inc(zeros_made, 1)

            @start.tensor
            def _(pe):
                pe.wait_ge(consts_loaded, 16)
                for c in range(NC):
                    if c % 2 == 0:
                        pe.wait_ge(x_in[c // 2], 16)
                    for h in range(2):
                        if c >= 4:
                            pe.wait_ge((start_left, start_right)[h], c - 3)
                        for k in range(4):
                            ins = pe.transpose(banks[2 * (c % 4) + h][:, k * P:(k + 1) * P],
                                               x[:, c, (4 * h + k) * P:(4 * h + k + 1) * P], ident)
                        ins.then_inc(start_turned, 1)

            @start.scalar
            def _(act):
                for c in range(NC):
                    act.wait_ge(start_turned, 2 * c + 1)
                    nc.scalar.activation(xT[:, 0:4, c * P:(c + 1) * P],
                                         banks[2 * (c % 4)][:, :].rearrange("p (k t) -> p k t", k=4), ACT.Copy).then_inc(start_left, 1)

            @start.vector
            def _(dve):
                for c in range(NC):
                    dve.wait_ge(start_turned, 2 * c + 2)
                    nc.vector.tensor_copy(xT[:, 4:8, c * P:(c + 1) * P],
                                          banks[2 * (c % 4) + 1][:, :].rearrange("p (k t) -> p k t", k=4)).then_inc(start_right, 1)

        with nc.Fori(0, DEPTH) as l:
            with nc.Block() as block:
                @block.sync
                def _(sp):
                    def load_unit(name, last, n):
                        s = n % SLOTS
                        tile_filled(sp, UNITS[n - SLOTS][1])
                        if name == "mem":
                            v = ring[:, s * 4096:(s + 1) * 4096].rearrange("p (m d) -> p m d", m=2 * MC)
                            sp.dma_start(v[:, 0:MC, :], mem_prompt[0].rearrange("(m p) d -> p m d", p=P)).then_inc(unit_loaded[s], 16)
                            sp.dma_start(v[:, MC:2 * MC, :], mem_sample[0].rearrange("(m p) d -> p m d", p=P)).then_inc(unit_loaded[s], 16)
                            return
                        w, off = {"mq": (w_in, OFF_MQ), "mv": (w_in, OFF_MV),
                                  "mo": (w_in, OFF_MO), "wo0": (w_out, 0), "wo1": (w_out, 512), "wk0": (wkv_mem, 0),
                                  "wk1": (wkv_mem, 512), "wv0": (wkv_mem, 1024), "wv1": (wkv_mem, 1536),
                                  "wq0": (wq_mem, 0), "wq1": (wq_mem, 512), "wx0": (wo_mem, 0), "wx1": (wo_mem, 512)}[name]
                        src = w[l].rearrange("(k p) n -> p k n", p=P)[:, :, off:off + 512]
                        v = unit_view(name, 512)
                        for h in range(2):
                            sp.dma_start(v[:, 4 * h:4 * h + 4, :], src[:, 4 * h:4 * h + 4, :]).then_inc(unit_loaded[s], 16)

                    for n, (name, last) in enumerate(UNITS[AHEAD:], AHEAD):
                        load_unit(name, last, n)
                        if n == AHEAD + 1:
                            sp.wait_ge(zeros_made, 1)
                            with sp.If(l < 1):
                                for slots in (slots_x, slots_y):
                                    for h in range(2):
                                        sp.dma_start(slots.rearrange("(b p) (h d) -> p b h d", p=P, h=2)[:, :, h, :],
                                                     zero_rows.unsqueeze(1).broadcast_to([P, XBLOCKS, 512])).then_inc(zeros_stored, 16)

                    sp.wait_ge(ids_ready, 1)
                    n_blocks = sp.value_load(r_nbi[0:1, 0:1], min_val=1, max_val=BLOCKS)
                    tile_filled(sp, UNITS[-1][1])
                    sp.wait_ge(scattered, l * (16 * 2 * NC) + 16 * 2 * NC)
                    sp.dma_start(xb, slots_x[0:P, :]).then_inc(x_loaded, 16)
                    gs, us, ds = 2, 0, 1
                    with sp.Fori(0, n_blocks) as b:
                        e = sp.value_load(r_bei[0:1, bass.ds(b, 1)], min_val=0, max_val=NE - 1)
                        wv = ring[:, gs * 4096:(gs + 1) * 4096].rearrange("p (k n) -> p k n", k=KD)
                        sp.wait_ge(g_filled, b + 1)
                        sp.dma_start(wv, w_gate[l, e].rearrange("(k p) n -> p k n", p=P)).then_inc(g_loaded, 16)
                        wv = ring[:, us * 4096:(us + 1) * 4096].rearrange("p (k n) -> p k n", k=KD)
                        sp.wait_ge(u_filled, b + 1)
                        sp.dma_start(wv, w_up[l, e].rearrange("(k p) n -> p k n", p=P)).then_inc(u_loaded, 16)
                        sp.wait_ge(xT_filled, 2 * b + 2)
                        sp.dma_start(xb, slots_x.rearrange("(b p) d -> b p d", p=P)[b + 1]).then_inc(x_loaded, 16)
                        wv = ring[:, ds * 4096:(ds + 1) * 4096].rearrange("p (k n) -> p k n", k=4)
                        sp.wait_ge(y_filled, 2 * b + 1)
                        sp.dma_start(wv, w_down[l, e].rearrange("(k p) n -> p k n", p=P)).then_inc(d_loaded, 16)
                    with sp.If(l < DEPTH - 1):
                        sp.wait_ge(ln_gained, 2)
                        sp.wait_ge(g_filled, n_blocks + 1)
                        sp.wait_ge(u_filled, n_blocks + 1)
                        sp.wait_ge(y_filled, 2 * n_blocks + 1)
                        load_ahead(sp, nc.s_assert_within(l + 1, 1, DEPTH - 1, skip_runtime_bounds_check_because="only before the last layer"))
                    with sp.If(l > DEPTH - 2):
                        for c in range(NC):
                            out = (y_prompt, y_sample)[SEQ_OF[c]]
                            sp.wait_ge(x_out, c + 1)
                            sp.dma_start(out[0].rearrange("(c p) d -> c p d", p=P)[c - BASE[SEQ_OF[c]]], x[:, c, :]).then_inc(out_stored, 16)

                @block.gpsimd
                def _(pool):
                    nc.gpsimd.memset(va[:, :, :, MD:MD + 1], 1.0).then_inc(ones_made, 1)
                    m = 0
                    for g, (h, s) in enumerate(ML_GROUPS):
                        for sc in range(CHUNKS[s]):
                            for d in range(2):
                                pool.wait_ge(d_exp, m + 1)
                                diag = dec[:, m // 2 % 2, d, 0:P] if d == 0 else dec[:, m // 2 % 2, d, sc * P:(sc + 1) * P]
                                sign = 1 if d == 0 else -1
                                nc.gpsimd.affine_select(out=diag, in_=diag, compare_op=ALU.is_ge, fill=0.0, base=0,
                                                        pattern=[[sign, P]], channel_multiplier=-sign).then_inc(d_masked, 1)
                                m += 1
                    pool.wait_ge(slots_ready, 1)
                    pool.wait_ge(zeros_stored, 64)
                    for a in range(2):
                        for c in range(NC):
                            nc.gpsimd.indirect_dma_start(
                                slots_x[:, :], bass.IndirectOffsetOnAxis(ap=slot_ids[:, a * NC + c:a * NC + c + 1].bitcast(U32), axis=0),
                                x[:, c, :], None).then_inc(scattered, 16)
                    pool.wait_ge(ids_ready, 1)
                    n_blocks = pool.value_load(r_nbi[0:1, 0:1], min_val=1, max_val=BLOCKS)
                    pool.wait_ge(y_stored, 16 * n_blocks + 16)
                    pool.sem_inc(all_stored, 1)
                    pool.wait_ge(all_stored, 1)
                    for c in range(NC):
                        for a in range(2):
                            nc.gpsimd.indirect_dma_start(
                                gath[:, a, c, :], None, slots_y[:, :],
                                bass.IndirectOffsetOnAxis(ap=slot_ids[:, a * NC + c:a * NC + c + 1].bitcast(U32), axis=0)).then_inc(gathered[c], 16)
                    pool.wait_ge(ln_rows_loaded[2], 32)
                    for c in range(NC):
                        pool.wait_ge(ln_scaled, c + 1)
                        nc.gpsimd.tensor_tensor(x[:, c, :], x[:, c, :], lnb, ALU.add).then_inc(x_out, 1)

                @block.scalar
                def _(act):
                    steps = [0]

                    def step(ins):
                        steps[0] += 1
                        ins.then_inc(act_done, 1)
                        act.wait_ge(act_done, steps[0])

                    signals = {}

                    def own(sem_):
                        signals[sem_.name] = signals.get(sem_.name, 0) + 1
                        act.wait_ge(sem_, signals[sem_.name])

                    def rstd(out, var, n, scale, eps):
                        step(nc.scalar.activation(out, var, ACT.Ln, bias=eps, scale=scale))
                        return nc.scalar.activation(out, out, ACT.Exp, scale=-0.5)

                    def drain_copy(key, out, cols, parts=P):
                        tile_filled(act, key)
                        nc.scalar.activation(out, bank_of(key)[0:parts, 0:cols], ACT.Copy).then_inc(drain_sem(key), 1)
                        tile_drained(act, key)

                    act.preload_act_table_set("natural_log_exp_and_others")
                    for dst, src in ((gbias[:, :], gate_bias), (sink[:, :], attn_sink), (gmix[:, 0:ATT], attn_norm_g),
                                     (gmix[:, ATT:D], mlstm_norm_g)):
                        act.dma_start(dst, src[l].partition_broadcast(P)).then_inc(rows_loaded, 16)
                    act.dma_start(z[0:24, 0:P], conv_w[l].rearrange("t (j p) -> (t j) p", p=P)).then_inc(taps_loaded, 16)
                    act.dma_start(z[24:32, 0:P], conv_b[l].rearrange("(j p) -> j p", p=P)).then_inc(taps_loaded, 16)

                    for c in range(NC):
                        tile_filled(act, ("q", c))
                        nc.scalar.activation(y[:, c, 0:ATT].rearrange("p (j t d) -> p t j d", j=GRP, t=NKV),
                                             bank_of(("q", c))[:, :].rearrange("p (t j d) -> p t j d", j=GRP, t=NKV),
                                             ACT.Copy).then_inc(drain_sem(("q", c)), 1)
                        tile_drained(act, ("q", c))
                    drain_copy(("gi",), rows[:, 0, 0:512], 512, 8)
                    drain_copy(("gf",), rows[:, 1, 0:512], 512, 8)
                    tile_filled(act, ("gs",))
                    step(nc.scalar.activation(rows[:, 0, 512:T], bank_of(("gs",))[0:8, 0:256], ACT.Copy))
                    nc.scalar.activation(rows[:, 1, 512:T], bank_of(("gs",))[0:8, 256:512], ACT.Copy).then_inc(drain_sem(("gs",)), 1)
                    tile_drained(act, ("gs",))
                    tile_drained(act, ("gf",))
                    tile_drained(act, ("gs",))
                    step(nc.scalar.activation(rows[:, 2, :], rows[:, 1, :], ACT.Abs))
                    step(nc.scalar.activation(rows[:, 2, :], rows[:, 2, :], ACT.Exp, scale=-1.0))
                    nc.scalar.activation(rows[:, 2, :], rows[:, 2, :], ACT.Ln, bias=one[0:8, :]).then_inc(lf_part, 1)
                    own(lf_part)
                    for c in range(NC):
                        key = ("qt", c)
                        tile_filled(act, key)
                        nc.scalar.activation(qT[:, :, c * P:(c + 1) * P],
                                             bank_of(key)[:, :].rearrange("p (j t) -> p j t", j=GRP), ACT.Copy).then_inc(drain_sem(key), 1)
                        tile_drained(act, key)
                    act.wait_ge(z_ready, 1)
                    nc.scalar.activation(rows[:, 5, :], rows[:, 5, :], ACT.Exp, scale=-1.0).then_inc(z_ready, 1)
                    act.wait_ge(z_ready, 2)

                    def stream_tile(key):
                        if key[0] == "cv":
                            i = STREAM.index(key)
                            n = SEQS[key[2]]
                            lo = BASE[key[2]] * P
                            tile_drained(act, key)
                            if i:
                                act.wait_ge(cv_used, i)
                            nc.scalar.activation(esc[:, 0:n], conv[:, key[1], lo:lo + n], ACT.Exp, scale=-1.0).then_inc(cv_exp, 1)
                            own(cv_exp)
                        elif key[0] == "v":
                            tile_filled(act, key)
                            nc.scalar.activation(va[:, key[1], :, 0:MD], bank_of(key)[:, :].rearrange("p (h d) -> p h d", h=MH),
                                                 ACT.Copy).then_inc(drain_sem(key), 1)
                            tile_drained(act, key)
                        else:
                            tile_filled(act, key)
                            if key[1] == NC - 1:
                                act.wait_ge(zeros_stored, 64)
                            nc.scalar.activation(y[:, key[1], ATT:D], bank_of(key)[:, :], ACT.Exp, scale=-1.0).then_inc(drain_sem(key), 1)
                            tile_drained(act, key)

                    def square_of(c):
                        tile_drained(act, ("pv", 2 * c + 1))
                        act.wait_ge(cv_used, 16)
                        step(nc.scalar.activation(esc[:, :], y[:, c, 0:ATT], ACT.Square, accum_out=st[:, 20 + c:21 + c]))

                    for i in range(13):
                        w = slot_tiles(i)
                        if i:
                            n = keys_of(GROUP_ORDER[i - 1][0])[1] * P
                            for j in range(GRP):
                                key = ("pt", i - 1, j)
                                tile_filled(act, key)
                                nc.scalar.activation(ptb[:, j, 0:n], bank_of(key)[:, 0:n], ACT.Copy).then_inc(drain_sem(key), 1)
                                tile_drained(act, key)
                        if i < 12:
                            nk = keys_of(GROUP_ORDER[i][0])[1] * P
                            act.wait_ge(m_ready, i + 1)
                            for j in range(GRP):
                                nc.scalar.activation(probs[:, j, 0:nk], probs[:, j, 0:nk], ACT.Exp, bias=st[:, 4 + j:5 + j],
                                                     accum_out=st[:, 8 + j:9 + j])
                            nc.scalar.activation(st[:, 12:16], st[:, 12:16], ACT.Exp).then_inc(p_ready, 1)
                            own(p_ready)
                        for t in slot_tiles(i - 1)[-1:] + w[:-1]:
                            stream_tile(t)
                        if i >= 8:
                            square_of(i - 8)
                    square_of(NC - 1)
                    rstd(st[:, 20:26], st[:, 20:26], 6, 1.0 / ATT, eps_rms).then_inc(att_rs, 1)
                    own(att_rs)
                    def drain_turned(key, c, h):
                        tile_filled(act, key)
                        nc.scalar.activation(xT[:, 4 * h:4 * h + 4, c * P:(c + 1) * P],
                                             bank_of(key)[:, :].rearrange("p (k t) -> p k t", k=4), ACT.Copy).then_inc(drain_sem(key), 1)
                        tile_drained(act, key)

                    pairs = []
                    for g in range(10):
                        if g < 8:
                            h, s = ML_GROUPS[g]
                            n = CHUNKS[s]
                            for d in range(2):
                                key = ("rb", g, d)
                                tile_filled(act, key)
                                nc.scalar.activation(rbc[:, d, 0:n * P], bank_of(key)[:, 0:n * P], ACT.Copy).then_inc(drain_sem(key), 1)
                                tile_drained(act, key)
                            tile_drained(act, ("rb", g, 0))
                            tile_drained(act, ("rb", g, 1))
                            for sc in range(n):
                                for d in range(2):
                                    if len(pairs) >= 2 and d == 0:
                                        act.wait_ge(sw_ready, len(pairs) - 1)
                                    if len(pairs) >= 2 and d == 1:
                                        tile_drained(act, pairs[-2])
                                    lo, hi = (sc, n) if d == 0 else (0, sc + 1)
                                    col = (BASE[s] + sc) * 8 + 4 * d + h
                                    nc.scalar.activation(dec[:, len(pairs) % 2, d, 0:(hi - lo) * P], rbc[:, d, lo * P:hi * P], ACT.Exp,
                                                         scale=-1.0, bias=zn[:, col:col + 1]).then_inc(d_exp, 1)
                                    own(d_exp)
                                pairs.append(("st", g, sc))
                        if g == 0:
                            for c in range(NC):
                                drain_turned(("yt", c, 0), c, 0)
                        if g >= 2:
                            gg = g - 2
                            h, s = ML_GROUPS[gg]
                            n = CHUNKS[s]
                            tile_drained(act, ("nm", gg, n - 1))
                            b = 30 + 4 * (gg % 2)
                            for t in range(n):
                                step(nc.scalar.activation(esc[:, 0:P], hsc[:, gg % 2, t, :], ACT.Square,
                                                          accum_out=st[:, b + t:b + t + 1]))
                            rstd(st[:, b:b + n], st[:, b:b + n], n, 1.0 / MD, eps_rms).then_inc(h_rs, 1)
                            own(h_rs)
                    def load_ln(i, g_, b_):
                        act.dma_start(lng, g_[l].partition_broadcast(P)).then_inc(ln_rows_loaded[i], 16)
                        act.dma_start(lnb, b_[l].partition_broadcast(P)).then_inc(ln_rows_loaded[i], 16)

                    def ln_scale(i):
                        act.wait_ge(ln_var, i + 1)
                        c = 40 + 2 * (i % 2)
                        rstd(st[:, c + 1:c + 2], st[:, c + 1:c + 2], 1, 1.0, eps_ln).then_inc(ln_rstd, 1)
                        own(ln_rstd)

                    for c in range(4):
                        drain_turned(("yt", c, 1), c, 1)
                    act.wait_ge(y_ml, 8)
                    load_ln(0, ln1_g, ln1_b)
                    for c in (4, 5):
                        drain_turned(("yt", c, 1), c, 1)
                    ln_scale(0)
                    ln_scale(1)
                    for k in range(KD):
                        key = ("mt", k)
                        tile_filled(act, key)
                        nc.scalar.activation(memT_hi[:, k, :], bank_of(key)[:, :], ACT.Copy).then_inc(mem_hi, 1)
                        own(mem_hi)
                        if k == 3:
                            ln_scale(2)
                    for c in range(3, NC - 1):
                        ln_scale(c)

                    def split_quarter(q):
                        n = UNIT[quarter_unit(q)]
                        if q % 2 == 0:
                            act.wait_ge(unit_loaded[n % SLOTS], 32 * (n // SLOTS))
                        tile_filled(act, ("wo", NC - 1, 1) if q == 1 else QUARTERS[q - 2][1] if q > 1 else ("mt", KD - 1))
                        nc.scalar.activation(quarter_parts(q)[0], quarter_raw(q), ACT.Copy).then_inc(w_hi, 1)
                        own(w_hi)

                    split_quarter(0)
                    ln_scale(NC - 1)
                    split_quarter(1)
                    for q in range(8):
                        for key in QUARTERS[q]:
                            if key[0] == "km":
                                drain_copy(key, km[:, key[1], :], 512)
                            else:
                                tile_filled(act, key)
                                nc.scalar.activation(vm[:, 2 * key[2]:2 * key[2] + 2, 256 * key[1]:256 * key[1] + 256],
                                                     bank_of(key)[:, :].rearrange("p (m n) -> p m n", m=2), ACT.Copy).then_inc(drain_sem(key), 1)
                                tile_drained(act, key)
                        if q + 2 < 8:
                            split_quarter(q + 2)
                        if q == 1:
                            act.wait_ge(x_ready, NC)
                            load_ln(1, ln2_g, ln2_b)
                    for c in range(NC):
                        drain_turned(("x2", c, 0), c, 0)
                    for j in range(KD):
                        for s in range(2):
                            lo = BASE[s] * P
                            drain_copy(("qx", j, s), qx[:, j, lo:lo + SEQS[s]], SEQS[s])
                    def cross_tail(cp):
                        for m in range(0, 4, 2):
                            key = ("ox", cp, m)
                            tile_filled(act, key)
                            nc.scalar.activation(xT[:, 2 * m:2 * m + 2, cp * 256:(cp + 1) * 256],
                                                 bank_of(key)[:, :].rearrange("p (k t) -> p k t", k=2), ACT.Copy).then_inc(drain_sem(key), 1)
                            tile_drained(act, key)
                        if cp:
                            ln_scale(xl + 2 * cp - 2)
                            ln_scale(xl + 2 * cp - 1)

                    xl = 6
                    for i in range(12):
                        act.wait_ge(xm_ready, i + 1)
                        key = ("sx", i)
                        if i >= 2:
                            tile_filled(act, ("px", i - 2))
                        for h in range(2):
                            o = X_STATS[i % 3]
                            last = nc.scalar.activation(xp[:, i % 2, h * NMEM:(h + 1) * NMEM], bank_of(key)[:, h * NMEM:(h + 1) * NMEM],
                                                        ACT.Exp, scale=1.0 / 16.0, bias=st[:, o + h:o + h + 1],
                                                        accum_out=st[:, o + 2 + h:o + 3 + h])
                            if h == 0:
                                step(last)
                            else:
                                last.then_inc(drain_sem(key), 1)
                                tile_drained(act, key)
                        if i:
                            c, hp = X_ITEMS[i - 1]
                            key = ("px", i - 1)
                            tile_filled(act, key)
                            if (i - 1) % 4 == 0 and i > 1:
                                tile_filled(act, ("ox", (i - 1) // 4 - 1, 3))
                            nc.scalar.activation(xpt[:, 2 * hp:2 * hp + 2, :, (c % 2) * P:(c % 2 + 1) * P],
                                                 bank_of(key)[:, :].rearrange("p (h m t) -> p h m t", h=2, m=MC),
                                                 ACT.Copy).then_inc(drain_sem(key), 1)
                            tile_drained(act, key)
                        if i and (i - 1) % 4 == 3:
                            cross_tail((i - 1) // 4)
                    c, hp = X_ITEMS[11]
                    key = ("px", 11)
                    tile_filled(act, key)
                    nc.scalar.activation(xpt[:, 2 * hp:2 * hp + 2, :, P:2 * P],
                                         bank_of(key)[:, :].rearrange("p (h m t) -> p h m t", h=2, m=MC),
                                         ACT.Copy).then_inc(drain_sem(key), 1)
                    tile_drained(act, key)
                    cross_tail(2)
                    for key in ROUTER_ORDER:
                        if key[0] == "wx" and key[2] == 0:
                            ln_scale(xl + key[1])
                        elif key[0] == "x3":
                            drain_turned(key, key[1], key[2])
                        elif key[0] == "rl":
                            c0, n = ROUTER_PARTS[key[1]]
                            tile_filled(act, key)
                            nc.scalar.activation(rrow[0:NE, c0 * P:(c0 + n) * P], bank_of(key)[0:NE, 0:n * P], ACT.Exp,
                                                 scale=-1.0).then_inc(drain_sem(key), 1)
                            tile_drained(act, key)
                    act.wait_ge(x_ready, 2 * NC)
                    load_ln(2, ln3_g, ln3_b)
                    act.wait_ge(ids_ready, 1)
                    n_blocks = act.value_load(r_nbi[0:1, 0:1], min_val=1, max_val=BLOCKS)
                    act.sem_inc(g_ready, 1)
                    act.sem_inc(yl_ready, 1)
                    act.sem_inc(y_stored, 16)

                    def block_xT():
                        nc.scalar.activation(xbT[:, 0:4, :], banks[0][:, :].rearrange("p (k t) -> p k t", k=4), ACT.Copy)
                        nc.scalar.activation(xbT[:, 4:8, :], banks[1][:, :].rearrange("p (k t) -> p k t", k=4),
                                             ACT.Copy).then_inc(xT_ready, 1)
                        own(xT_ready)

                    act.preload_act_table(ACT.Silu)
                    act.wait_ge(xT_filled, 2)
                    block_xT()
                    with act.Fori(0, n_blocks) as b:
                        act.wait_ge(h_done, b + 1)
                        act.wait_ge(g_filled, b + 2)
                        nc.scalar.activation(gact, banks[2][:, :], ACT.Silu).then_inc(g_ready, 1)
                        act.wait_ge(hTl_filled, b + 1)
                        nc.scalar.activation(hbT[:, 0:2, :], banks[4][:, 0:256].rearrange("p (k t) -> p k t", k=2), ACT.Copy).then_inc(hTl_ready, 1)
                        act.wait_ge(xT_filled, 2 * b + 4)
                        block_xT()
                        act.wait_ge(hT_filled, b + 1)
                        nc.scalar.activation(hbT[:, 2:4, :], banks[3][:, 256:512].rearrange("p (k t) -> p k t", k=2), ACT.Copy).then_inc(hT_ready, 1)
                        act.wait_ge(y_stored, 16 * b + 16)
                        act.wait_ge(y_filled, 2 * b + 2)
                        nc.scalar.activation(yb[:, 0:512], banks[5][:, :], ACT.Copy).then_inc(yl_ready, 1)
                        act.wait_ge(yl_ready, b + 2)
                        act.wait_ge(yr_ready, b + 2)
                        act.dma_start(slots_y.rearrange("(b p) d -> b p d", p=P)[b], yb).then_inc(y_stored, 16)
                    act.preload_act_table_set("natural_log_exp_and_others")
                    for c in range(NC + 1):
                        if c < NC:
                            ln_scale(12 + c)
                            act.wait_ge(ln_gained, c + 1)
                            o = 40 + 2 * (c % 2)
                            nc.scalar.activation(x[:, c, :], x[:, c, :], ACT.Copy, scale=st[:, o + 1:o + 2]).then_inc(ln_scaled, 1)
                        if c:
                            for h in range(2):
                                key = ("xn", c - 1, h)
                                tile_filled(act, key)
                                nc.scalar.activation(xT[:, 4 * h:4 * h + 4, (c - 1) * P:c * P],
                                                     bank_of(key)[:, :].rearrange("p (k t) -> p k t", k=4), ACT.Copy).then_inc(drain_sem(key), 1)
                                tile_drained(act, key)

                @block.vector
                def _(dve):
                    steps = [0]

                    def step(ins):
                        steps[0] += 1
                        ins.then_inc(dve_done, 1)
                        dve.wait_ge(dve_done, steps[0])

                    signals = {}

                    def own(sem_):
                        signals[sem_.name] = signals.get(sem_.name, 0) + 1
                        dve.wait_ge(sem_, signals[sem_.name])

                    v = nc.vector

                    def drain_xT(key, c):
                        tile_filled(dve, key)
                        v.tensor_copy(xT[:, 4:8, c * P:(c + 1) * P],
                                      bank_of(key)[:, :].rearrange("p (k t) -> p k t", k=4)).then_inc(drain_sem(key), 1)
                        tile_drained(dve, key)

                    v.memset(rows[:, 7, :], 1.0)
                    dve.wait_ge(rows_loaded, 4 * 16)
                    for c in range(NC):
                        key = ("kvg", c)
                        tile_filled(dve, key)
                        v.tensor_copy(kv[:, c, :], bank_of(key)[:, 0:256])
                        v.tensor_tensor(gts[:, c * NG:(c + 1) * NG].rearrange("p (g d h) -> p d g h", g=2, d=2),
                                        bank_of(key)[:, 256:272].rearrange("p (d g h) -> p d g h", g=2, d=2),
                                        gbias[:, :].rearrange("p (d g h) -> p d g h", g=2, d=2), ALU.add).then_inc(drain_sem(key), 1)
                        tile_drained(dve, key)
                    tile_drained(dve, ("kvg", NC - 1))

                    def rope(view, heads):
                        n = NC * heads * HALF
                        shape = [P, NC, heads, HALF]
                        t = [z[:, 1024 + a * n:1024 + (a + 1) * n].rearrange("p (c h d) -> p c h d", c=NC, h=heads) for a in range(4)]
                        cos, sin = (cst[:, o:o + NC * HALF].rearrange("p (c d) -> p c d", c=NC).unsqueeze(2).broadcast_to(shape)
                                    for o in (C_COS, C_SIN))
                        x1, x2 = view[:, :, :, 0:HALF], view[:, :, :, HALF:ROT]
                        v.tensor_tensor(t[0], x1, cos, ALU.mult)
                        v.tensor_tensor(t[1], x2, sin, ALU.mult)
                        v.tensor_tensor(t[2], x2, cos, ALU.mult)
                        step(v.tensor_tensor(t[3], x1, sin, ALU.mult))
                        v.tensor_tensor(x1, t[0], t[1], ALU.subtract)
                        return v.tensor_tensor(x2, t[2], t[3], ALU.add)

                    k_heads = kv[:, :, 0:NKV * HD].rearrange("p c (h d) -> p c h d", h=NKV)
                    rope(k_heads, NKV).then_inc(k_roped, 1)
                    own(k_roped)
                    tile_drained(dve, ("q", NC - 1))
                    q_heads = y[:, :, 0:ATT].rearrange("p c (h d) -> p c h d", h=NH)
                    rope(q_heads, NH).then_inc(q_roped, 1)
                    own(q_roped)
                    for key, lo, n in ((("kt0",), 0, 512), (("kt1",), 512, 256)):
                        tile_filled(dve, key)
                        v.tensor_copy(kT[:, lo:lo + n], bank_of(key)[:, 0:n]).then_inc(drain_sem(key), 1)
                        tile_drained(dve, key)
                    tile_filled(dve, ("cw",))
                    v.tensor_copy(cwb[:, :], bank_of(("cw",))[:, 0:32]).then_inc(drain_sem(("cw",)), 1)
                    tile_drained(dve, ("cw",))

                    dve.wait_ge(lf_part, 1)
                    r = [rows[:, j, :] for j in range(8)]
                    fwd, bwd = cst[0:8, C_FWD:C_FWD + 1], cst[0:8, C_BWD:C_BWD + 1]
                    step(v.scalar_tensor_tensor(out=r[1], in0=r[1], scalar=0.0, in1=r[2], op0=ALU.min, op1=ALU.subtract))

                    def scans(src_a, src_b, op0, op1, out):
                        for lo, n in ((0, 512), (512, 256)):
                            w = slice(lo, lo + n)
                            v.tensor_tensor_scan(r[2][:, w], src_a[:, w], src_b[:, w], 0.0, op0, op1)
                            back = slice(lo + n - 1, lo - 1 if lo else None, -1)
                            step(v.tensor_tensor_scan(r[6][:, back], src_a[:, back], src_b[:, back], 0.0, op0, op1))
                        step(v.tensor_scalar(r[6], r[6], bwd, None, ALU.mult))
                        step(v.scalar_tensor_tensor(out=out, in0=r[2], scalar=fwd, in1=r[6], op0=ALU.mult, op1=ALU.add))

                    scans(r[7], r[1], ALU.mult, ALU.add, r[3])
                    step(v.tensor_tensor(r[4], r[0], r[3], ALU.subtract))
                    scans(r[4], r[4], ALU.max, ALU.max, rrow[0:8, :])
                    v.tensor_tensor(r[5], r[3], rrow[0:8, :], ALU.add).then_inc(z_ready, 1)
                    own(z_ready)

                    def conv_finish(i):
                        _, j, s = STREAM[i]
                        n, lo = SEQS[s], BASE[s] * P
                        dve.wait_ge(cv_exp, i + 1)
                        step(v.tensor_scalar(esc[:, 0:n], esc[:, 0:n], 1.0, None, ALU.add))
                        step(v.reciprocal(esc[:, 0:n], esc[:, 0:n]))
                        c_ = conv[:, j, lo:lo + n]
                        v.scalar_tensor_tensor(out=c_, in0=c_, scalar=1.0 if j < 4 else float(MD) ** -0.5, in1=esc[:, 0:n],
                                               op0=ALU.mult, op1=ALU.mult).then_inc(cv_used, 1)
                        own(cv_used)

                    def stream_tile(key):
                        i = STREAM.index(key)
                        if key[0] == "cv":
                            _, j, s = key
                            n, lo = SEQS[s], BASE[s] * P
                            ps = bank_of(key)
                            c_ = conv[:, j, lo:lo + n]
                            tile_filled(dve, key)
                            tap = [cwb[:, t * 8 + j:t * 8 + j + 1] for t in range(4)]
                            step(v.tensor_scalar(c_, ps[:, 0:n], tap[1], tap[3], ALU.mult, ALU.add))
                            step(v.scalar_tensor_tensor(out=c_[:, 1:n], in0=ps[:, 0:n - 1], scalar=tap[0], in1=c_[:, 1:n],
                                                        op0=ALU.mult, op1=ALU.add))
                            v.scalar_tensor_tensor(out=c_[:, 0:n - 1], in0=ps[:, 1:n], scalar=tap[2], in1=c_[:, 0:n - 1],
                                                   op0=ALU.mult, op1=ALU.add).then_inc(drain_sem(key), 1)
                            tile_drained(dve, key)
                        if 1 <= i <= 16:
                            conv_finish(i - 1)

                    def o_finish(key):
                        if key[0] == "o":
                            tile_drained(dve, key)
                            o_ = y[:, key[1], ATT:D]
                            step(v.tensor_scalar(o_, o_, 1.0, None, ALU.add))
                            step(v.reciprocal(o_, o_))
                            step(v.tensor_tensor(o_, o_, gmix[:, ATT:D], ALU.mult))

                    dve.wait_ge(taps_loaded, 32)
                    for i in range(13):
                        w = slot_tiles(i)
                        if i:
                            dve.wait_ge(p_ready, i)
                            ro = 110 + 4 * ((i - 1) % 2)
                            step(v.tensor_tensor(st[:, ro:ro + 4], st[:, 8:12], st[:, 12:16], ALU.add))
                            step(v.reciprocal(st[:, ro:ro + 4], st[:, ro:ro + 4]))
                        if i < 12:
                            c, n = GROUP_ORDER[i]
                            _, nb, m0 = keys_of(c)
                            nk = nb * P
                            if i:
                                tile_filled(dve, ("pt", i - 1, 3))
                            else:
                                tile_filled(dve, ("cw",))
                            for j in range(GRP):
                                key = ("sc", i, j)
                                tile_filled(dve, key)
                                v.scalar_tensor_tensor(out=probs[:, j, 0:nk], in0=bank_of(key)[:, 0:nk], scalar=HD ** -0.5,
                                                       in1=cst[:, C_MASK + m0:C_MASK + m0 + nk], op0=ALU.mult,
                                                       op1=ALU.add).then_inc(drain_sem(key), 1)
                                tile_drained(dve, key)
                            for j in range(GRP):
                                tile_drained(dve, ("sc", i, j))
                            step(v.tensor_reduce(st[:, 0:4], probs[:, :, 0:nk], AX.X, ALU.max))
                            sk = sink[:, n * GRP:(n + 1) * GRP]
                            step(v.tensor_tensor(st[:, 0:4], st[:, 0:4], sk, ALU.max))
                            v.tensor_scalar(st[:, 4:8], st[:, 0:4], -1.0, None, ALU.mult)
                            v.tensor_tensor(st[:, 12:16], sk, st[:, 0:4], ALU.subtract).then_inc(m_ready, 1)
                            own(m_ready)
                        for t in slot_tiles(i - 1)[-1:]:
                            o_finish(t)
                        if i == 0:
                            key = ("zt",)
                            tile_filled(dve, key)
                            v.tensor_copy(zn[:, :], bank_of(key)[:, 0:48])
                            v.tensor_copy(thr[:, :], bank_of(key)[:, 48:96]).then_inc(drain_sem(key), 1)
                            tile_drained(dve, key)
                        if w:
                            stream_tile(w[0])
                            o_finish(w[0])
                        if i:
                            c, n = GROUP_ORDER[i - 1]
                            key = ("pv", i - 1)
                            tile_filled(dve, key)
                            step_ = v.tensor_tensor(y[:, c, n * 256:(n + 1) * 256].rearrange("p (j d) -> p j d", j=GRP),
                                                    bank_of(key)[:, 0:256].rearrange("p (j d) -> p j d", j=GRP),
                                                    st[:, ro:ro + 4].unsqueeze(2).broadcast_to([P, GRP, HD]), ALU.mult)
                            step_.then_inc(drain_sem(key), 1)
                            tile_drained(dve, key)
                        for t in w[1:]:
                            stream_tile(t)
                        for t in w[1:-1]:
                            o_finish(t)
                    dve.wait_ge(att_rs, 1)
                    for c in range(NC):
                        v.scalar_tensor_tensor(out=y[:, c, 0:ATT], in0=y[:, c, 0:ATT], scalar=st[:, 20 + c:21 + c],
                                               in1=gmix[:, 0:ATT], op0=ALU.mult, op1=ALU.mult).then_inc(y_att, 1)
                        own(y_att)

                    m = 0
                    for g in range(10):
                        if g < 8:
                            h, s = ML_GROUPS[g]
                            n = CHUNKS[s]
                            for sc in range(n):
                                key = ("st", g, sc)
                                tile_filled(dve, key)
                                for d in range(2):
                                    dve.wait_ge(d_masked, m + 1)
                                    lo, hi = (sc, n) if d == 0 else (0, sc + 1)
                                    ins = v.tensor_tensor(sw_at(g, d, n, sc, lo, hi), bank_of(key)[:, lo * P:hi * P],
                                                          dec[:, m // 2 % 2, d, 0:(hi - lo) * P], ALU.mult)
                                    if d == 0:
                                        ins.then_inc(sw_ready, 1)
                                        own(sw_ready)
                                    else:
                                        ins.then_inc(drain_sem(key), 1)
                                        tile_drained(dve, key)
                                    m += 1
                        if 1 <= g < 9:
                            gg = g - 1
                            h, s = ML_GROUPS[gg]
                            for t in range(CHUNKS[s]):
                                key = ("nm", gg, t)
                                c = BASE[s] + t
                                tile_filled(dve, key)
                                ps = bank_of(key)[:, :].rearrange("p (d e) -> p d e", d=2)
                                floor = thr[:, c * 8:c * 8 + 8].rearrange("p (d h) -> p d h", d=2)[:, :, h:h + 1]
                                den = st[:, 100:102].rearrange("p (d e) -> p d e", d=2)
                                step(v.tensor_reduce(st[:, 100:102], ps[:, :, MD:MD + 1], AX.X, ALU.max, apply_absolute_value=True))
                                step(v.tensor_tensor(den, den, floor, ALU.max))
                                step(v.reciprocal(den, den))
                                hs = hsc[:, gg % 2, t, :]
                                step(v.tensor_scalar(hs, ps[:, 0, 0:MD], st[:, 100:101], None, ALU.mult))
                                v.scalar_tensor_tensor(out=hs, in0=ps[:, 1, 0:MD], scalar=st[:, 101:102], in1=hs,
                                                       op0=ALU.mult, op1=ALU.add).then_inc(drain_sem(key), 1)
                                tile_drained(dve, key)
                        if g >= 2:
                            gg = g - 2
                            h, s = ML_GROUPS[gg]
                            dve.wait_ge(h_rs, gg + 1)
                            b = 30 + 4 * (gg % 2)
                            for t in range(CHUNKS[s]):
                                o_ = y[:, BASE[s] + t, ATT + h * MD:ATT + (h + 1) * MD]
                                ins = v.scalar_tensor_tensor(out=o_, in0=hsc[:, gg % 2, t, :], scalar=st[:, b + t:b + t + 1],
                                                             in1=o_, op0=ALU.mult, op1=ALU.mult)
                            ins.then_inc(y_ml, 1)
                            own(y_ml)

                    def ln_stats(i, c):
                        o = 40 + 2 * (i % 2)
                        b = st[:, 70:82]
                        v.bn_stats(b[:, 0:6], x[:, c, 0:512])
                        step(v.bn_stats(b[:, 6:12], x[:, c, 512:D]))
                        v.bn_aggr(st[:, o:o + 2], b).then_inc(ln_var, 1)
                        own(ln_var)

                    def ln_apply(i, c):
                        o = 40 + 2 * (i % 2)
                        dve.wait_ge(ln_rows_loaded[i // NC], 32)
                        dve.wait_ge(ln_rstd, i + 1)
                        step(v.scalar_tensor_tensor(out=x[:, c, :], in0=x[:, c, :], scalar=st[:, o:o + 1], in1=lng,
                                                    op0=ALU.subtract, op1=ALU.mult))
                        v.scalar_tensor_tensor(out=x[:, c, :], in0=x[:, c, :], scalar=st[:, o + 1:o + 2], in1=lnb,
                                               op0=ALU.mult, op1=ALU.add).then_inc(x_ready, 1)
                        own(x_ready)

                    def residual_ln(i, c, name):
                        for h in range(2):
                            key = (name, c, h)
                            tile_filled(dve, key)
                            xh = x[:, c, 512 * h:512 * h + 512]
                            v.scalar_tensor_tensor(out=xh, in0=xh, scalar=ALPHA, in1=bank_of(key)[:, :],
                                                   op0=ALU.mult, op1=ALU.add).then_inc(drain_sem(key), 1)
                            tile_drained(dve, key)
                        tile_drained(dve, (name, c, 0))
                        tile_drained(dve, (name, c, 1))
                        ln_stats(i, c)
                        ln_apply(i, c)

                    def low_quarter(q):
                        dve.wait_ge(w_hi, q + 1)
                        hi, low = quarter_parts(q)
                        v.tensor_tensor(low, quarter_raw(q), hi.bitcast(F32), ALU.subtract).then_inc(w_lo, 1)
                        own(w_lo)

                    for c in range(NC):
                        residual_ln(c, c, "wo")
                        if c == 2:
                            for k in range(KD):
                                key = ("mt", k)
                                dve.wait_ge(mem_hi, k + 1)
                                v.tensor_tensor(memT_lo[:, k, :], bank_of(key)[:, :], memT_hi[:, k, :].bitcast(F32),
                                                ALU.subtract).then_inc(drain_sem(key), 1)
                                tile_drained(dve, key)
                        if c == NC - 2:
                            low_quarter(0)
                    for q in range(1, 8):
                        low_quarter(q)
                    for c in range(NC):
                        drain_xT(("x2", c, 1), c)

                    def cross_max(i):
                        o = X_STATS[i % 3]
                        key = ("sx", i)
                        tile_filled(dve, key)
                        step(v.tensor_reduce(st[:, o:o + 2], bank_of(key)[:, :].rearrange("p (h m) -> p h m", h=2), AX.X, ALU.max))
                        v.tensor_scalar(st[:, o:o + 2], st[:, o:o + 2], -float(XD) ** -0.5, None, ALU.mult).then_inc(xm_ready, 1)
                        own(xm_ready)

                    def cross_norm(i):
                        o = X_STATS[i % 3]
                        tile_drained(dve, ("sx", i))
                        step(v.reciprocal(st[:, o + 4:o + 6], st[:, o + 2:o + 4]))
                        for h in range(2):
                            ph = xp[:, i % 2, h * NMEM:(h + 1) * NMEM]
                            ins = v.tensor_scalar(ph, ph, st[:, o + 4 + h:o + 5 + h], None, ALU.mult)
                        ins.then_inc(xp_ready, 1)
                        own(xp_ready)

                    cross_max(0)
                    cross_max(1)
                    for i in range(12):
                        cross_norm(i)
                        if i + 2 < 12:
                            cross_max(i + 2)
                        if i % 4 == 3:
                            cp = i // 4
                            for mm in (1, 3):
                                key = ("ox", cp, mm)
                                tile_filled(dve, key)
                                v.tensor_copy(xT[:, 2 * mm:2 * mm + 2, cp * 256:(cp + 1) * 256],
                                              bank_of(key)[:, :].rearrange("p (k t) -> p k t", k=2)).then_inc(drain_sem(key), 1)
                                tile_drained(dve, key)
                            if cp:
                                for c in (2 * cp - 2, 2 * cp - 1):
                                    residual_ln(NC + c, c, "wx")
                    for c in (4, 5):
                        residual_ln(NC + c, c, "wx")

                    tile_filled(dve, ("rt",))
                    v.tensor_scalar(r_s, bank_of(("rt",))[:, 0:NS_], 1.0, None, ALU.add).then_inc(drain_sem(("rt",)), 1)
                    tile_drained(dve, ("rt",))
                    step(v.reciprocal(r_s, r_s))

                    def by_chunk(a):
                        return a.rearrange("p (c e) -> p c e", c=NC)

                    def to_chunks(a):
                        return a.unsqueeze(1).broadcast_to([P, NC, NE])

                    step(v.tensor_tensor(by_chunk(r_sel), by_chunk(r_s), to_chunks(rbias[:, :]), ALU.add))

                    def ranks(val, n, out):
                        b1, b2 = (a[:, 0:n * 16].rearrange("p (g i j) -> p g i j", i=4, j=4) for a in (r_beat, r_beat2))
                        four = [P, n, 4, 4]
                        vi = val.rearrange("p (g i) -> p g i", i=4).unsqueeze(3).broadcast_to(four)
                        vj = val.rearrange("p (g j) -> p g j", j=4).unsqueeze(2).broadcast_to(four)
                        tri = cst[:, C_TRI:C_TRI + 16].rearrange("p (i j) -> p i j", i=4).unsqueeze(1).broadcast_to(four)
                        v.tensor_tensor(b1, vj, vi, ALU.is_gt)
                        step(v.tensor_tensor(b2, vj, vi, ALU.is_equal))
                        step(v.tensor_tensor(b2, b2, tri, ALU.mult))
                        step(v.tensor_tensor(b1, b1, b2, ALU.add))
                        step(v.tensor_reduce(out, b1, AX.X, ALU.add))

                    ranks(r_sel, 24, r_rank)
                    step(v.tensor_scalar(r_m, r_rank, 1.5, None, ALU.is_lt))
                    step(v.tensor_tensor(r_t1, r_m, r_sel, ALU.mult))
                    step(v.tensor_reduce(r_gs, r_t1.rearrange("p (g i) -> p g i", i=4), AX.X, ALU.add))
                    ranks(r_gs, NC, r_gr)
                    step(v.tensor_scalar(r_gr, r_gr, 0.5, None, ALU.is_lt))
                    m_ = r_m.rearrange("p (g i) -> p g i", i=4)
                    v.tensor_tensor(m_, m_, r_gr.unsqueeze(2).broadcast_to([P, 24, 4]), ALU.mult).then_inc(mask_ready, 1)
                    own(mask_ready)
                    dve.wait_ge(mask_ready, 1)
                    key = ("rank",)
                    tile_filled(dve, key)
                    v.tensor_copy(r_slot, bank_of(key)[:, 0:NS_])
                    v.tensor_copy(r_tot, bank_of(key)[:, NS_:2 * NS_]).then_inc(drain_sem(key), 1)
                    tile_drained(dve, key)
                    step(v.memset(r_cnt, 0.0))
                    tile_drained(dve, key)
                    for c in range(NC):
                        sl = slice(c * NE, (c + 1) * NE)
                        step(v.tensor_tensor(r_slot[:, sl], r_slot[:, sl], r_cnt, ALU.add))
                        step(v.tensor_tensor(r_cnt, r_cnt, r_tot[:, sl], ALU.add))
                    cmp_ = r_cmp[:, 0:NE * NC].rearrange("p (e j) -> p e j", e=NE)
                    step(v.tensor_tensor(cmp_, r_cnt.unsqueeze(2).broadcast_to([P, NE, NC]),
                                         cst[:, C_STEP:C_STEP + NC].unsqueeze(1).broadcast_to([P, NE, NC]), ALU.is_gt))
                    step(v.tensor_reduce(r_nb, cmp_, AX.X, ALU.add))
                    step(v.tensor_tensor_scan(r_end, cst[:, C_ONES:C_ONES + NE], r_nb, 0.0, ALU.mult, ALU.add))
                    step(v.tensor_tensor(r_start, r_end, r_nb, ALU.subtract))
                    step(v.tensor_scalar(r_start, r_start, float(P), None, ALU.mult))
                    step(v.tensor_tensor(by_chunk(r_slot), by_chunk(r_slot), to_chunks(r_start), ALU.add))
                    sa, sb_ = r_slots[:, 0:NC], r_slots[:, NC:2 * NC]
                    step(v.tensor_tensor(r_t1, r_slot, r_m, ALU.mult))
                    step(v.tensor_reduce(sb_, by_chunk(r_t1), AX.X, ALU.max))
                    step(v.tensor_scalar(r_t1, r_slot, FAR, None, ALU.subtract))
                    step(v.tensor_tensor(r_t1, r_t1, r_m, ALU.mult))
                    step(v.tensor_scalar(r_t1, r_t1, FAR, None, ALU.add))
                    step(v.tensor_reduce(sa, by_chunk(r_t1), AX.X, ALU.min))
                    v.tensor_copy(slot_ids, r_slots).then_inc(slots_ready, 1)
                    cmp_ = r_cmp[:, :].rearrange("p (b e) -> p b e", e=NE)
                    shape = [P, XBLOCKS, NE]
                    step(v.tensor_tensor(cmp_, cst[:, C_IOTA:C_IOTA + XBLOCKS].unsqueeze(2).broadcast_to(shape),
                                         r_end.unsqueeze(1).broadcast_to(shape), ALU.is_ge))
                    step(v.tensor_reduce(r_be, cmp_, AX.X, ALU.add))
                    v.tensor_scalar(r_bei, r_be, float(NE - 1), None, ALU.min)
                    v.tensor_copy(r_nbi, r_end[:, NE - 1:NE]).then_inc(ids_ready, 1)
                    own(ids_ready)
                    step(v.tensor_tensor(r_w, r_s, r_m, ALU.mult))
                    step(v.tensor_reduce(r_sum, by_chunk(r_w), AX.X, ALU.add))
                    step(v.reciprocal(r_sum, r_sum))
                    step(v.tensor_tensor(by_chunk(r_w), by_chunk(r_w), r_sum.unsqueeze(2).broadcast_to([P, NC, NE]), ALU.mult))
                    for a, s_ in ((0, sa), (1, sb_)):
                        step(v.tensor_tensor(by_chunk(r_t1), by_chunk(r_slot), s_.unsqueeze(2).broadcast_to([P, NC, NE]), ALU.is_equal))
                        step(v.tensor_tensor(r_t1, r_t1, r_w, ALU.mult))
                        step(v.tensor_reduce(gw[:, a * NC:(a + 1) * NC], by_chunk(r_t1), AX.X, ALU.add))
                    dve.wait_ge(scattered, l * (16 * 2 * NC) + 16 * 2 * NC)
                    for c in range(NC):
                        step(v.tensor_scalar(x[:, c, :], x[:, c, :], ALPHA, None, ALU.mult))
                    dve.wait_ge(ids_ready, 1)
                    n_blocks = dve.value_load(r_nbi[0:1, 0:1], min_val=1, max_val=BLOCKS)
                    dve.sem_inc(h_done, 1)
                    dve.sem_inc(yr_ready, 1)
                    with dve.Fori(0, n_blocks) as b:
                        dve.wait_ge(g_ready, b + 2)
                        dve.wait_ge(ul_filled, b + 1)
                        v.tensor_tensor(hb[:, 0:256], gact[:, 0:256], banks[3][:, 0:256], ALU.mult).then_inc(hl_done, 1)
                        dve.wait_ge(u_filled, b + 2)
                        v.tensor_tensor(hb[:, 256:512], gact[:, 256:512], banks[7][:, 0:256], ALU.mult).then_inc(h_done, 1)
                        dve.wait_ge(y_stored, 16 * b + 16)
                        dve.wait_ge(y_filled, 2 * b + 3)
                        v.tensor_copy(yb[:, 512:D], banks[6][:, :]).then_inc(yr_ready, 1)
                    dve.wait_ge(ln_rows_loaded[2], 32)
                    for c in range(NC):
                        dve.wait_ge(gathered[c], l * 32 + 32)
                        xc = x[:, c, :]
                        for a in range(2):
                            step(v.scalar_tensor_tensor(out=xc, in0=gath[:, a, c, :], scalar=gw[:, a * NC + c:a * NC + c + 1],
                                                        in1=xc, op0=ALU.mult, op1=ALU.add))
                        if c >= 2:
                            dve.wait_ge(ln_scaled, c - 1)
                        ln_stats(2 * NC + c, c)
                        o = 40 + 2 * (c % 2)
                        v.scalar_tensor_tensor(out=xc, in0=xc, scalar=st[:, o:o + 1], in1=lng,
                                               op0=ALU.subtract, op1=ALU.mult).then_inc(ln_gained, 1)

                @block.tensor
                def _(pe):
                    def take(key):
                        b, use = TILES[key]
                        if use:
                            pe.wait_ge(drained[b], use)
                        return banks[b]

                    def done(ins, key):
                        ins.then_inc(filled[TILES[key][0]], 1)

                    def unit_ready(name):
                        n = UNIT[name]
                        if n < AHEAD:
                            pe.wait_ge(ahead[n], l * 32 + 32)
                        else:
                            pe.wait_ge(unit_loaded[n % SLOTS], 32 * (n // SLOTS))

                    def turn4(key, source):
                        ps = take(key)
                        for k in range(4):
                            ins = pe.transpose(ps[:, k * P:(k + 1) * P], source(k), ident)
                        done(ins, key)

                    def product(key, n, lhs, rhs, ks=KD):
                        ps = take(key)
                        for k in range(ks):
                            ins = pe.matmul(ps[:, 0:n], lhs(k), rhs(k), start=(k == 0), stop=(k == ks - 1))
                        done(ins, key)

                    unit_ready("kvg")
                    wv = unit_view("kvg", 272)
                    for c in range(NC):
                        product(("kvg", c), 272, lambda k: xT[:, k, c * P:(c + 1) * P], lambda k: wv[:, k, :])
                    unit_ready("q")
                    wv = unit_view("q", 512)
                    for c in range(NC):
                        product(("q", c), 512, lambda k: xT[:, k, c * P:(c + 1) * P], lambda k: wv[:, k, :])
                    tile_drained(pe, ("kvg", NC - 1))

                    def gate_cols(c, g):
                        return gts[:, c * NG + 8 * g:c * NG + 8 * g + 8]

                    for name, g in (("gi", 0), ("gf", 1)):
                        ps = take((name,))
                        for c in range(4):
                            ins = pe.transpose(ps[0:8, c * P:(c + 1) * P], gate_cols(c, g), ident)
                        done(ins, (name,))
                    ps = take(("gs",))
                    for g in range(2):
                        for c in (4, 5):
                            o = g * 256 + (c - 4) * P
                            ins = pe.transpose(ps[0:8, o:o + P], gate_cols(c, g), ident)
                    done(ins, ("gs",))
                    pe.wait_ge(k_roped, 1)
                    for name, cs in (("kt0", range(0, 4)), ("kt1", range(4, 6))):
                        ps = take((name,))
                        for c in cs:
                            o = (c - cs[0]) * P
                            ins = pe.transpose(ps[:, o:o + P], kv[:, c, 0:P], ident)
                        done(ins, (name,))
                    pe.wait_ge(q_roped, 1)
                    for c in range(NC):
                        turn4(("qt", c), lambda k: y[:, c, k * P:(k + 1) * P])
                    pe.wait_ge(taps_loaded, 32)
                    ps = take(("cw",))
                    done(pe.transpose(ps[:, 0:32], z[0:32, 0:P], ident[0:32, 0:32]), ("cw",))
                    def turn_gates():
                        pe.wait_ge(z_ready, 2)
                        ps = take(("zt",))
                        for a, row in ((0, 4), (1, 5)):
                            for c in range(NC):
                                o = a * 48 + c * 8
                                ins = pe.transpose(ps[:, o:o + 8], rows[:, row, c * P:(c + 1) * P], ident[0:8, 0:8])
                        done(ins, ("zt",))

                    def stream_tile(key):
                        if key[0] == "cv":
                            _, j, s = key
                            name = "mq" if j < 4 else "mk"
                            unit_ready(name)
                            w = unit_view(name, 512)
                            jj, lo = j % 4, BASE[s] * P
                            product(key, SEQS[s], lambda k: w[:, k, jj * P:(jj + 1) * P], lambda k: xT[:, k, lo:lo + SEQS[s]])
                        else:
                            name = "mv" if key[0] == "v" else "mo"
                            unit_ready(name)
                            w = unit_view(name, 512)
                            c = key[1]
                            product(key, 512, lambda k: xT[:, k, c * P:(c + 1) * P], lambda k: w[:, k, :])

                    tile_drained(pe, ("qt", NC - 1))
                    tile_drained(pe, ("kt1",))
                    for i in range(13):
                        w = slot_tiles(i)

                        def turn_probs(j):
                            c, _ = GROUP_ORDER[i - 1]
                            nb = keys_of(c)[1]
                            key = ("pt", i - 1, j)
                            ps = take(key)
                            for k in range(nb):
                                ins = pe.transpose(ps[:, k * P:(k + 1) * P], probs[:, j, k * P:(k + 1) * P], ident)
                            done(ins, key)

                        if i < 12:
                            c, n = GROUP_ORDER[i]
                            k0, nb, _ = keys_of(c)
                            hp = slice(n * HD, (n + 1) * HD)
                            for j in range(GRP):
                                key = ("sc", i, j)
                                ps = take(key)
                                done(pe.matmul(ps[:, 0:nb * P], qT[hp, j, c * P:(c + 1) * P], kT[hp, k0 * P:(k0 + nb) * P],
                                               start=True, stop=True), key)
                        if i:
                            pe.wait_ge(p_ready, i)
                            for j in range(GRP):
                                turn_probs(j)
                        if w:
                            stream_tile(w[0])
                        if i == 0:
                            turn_gates()
                        if i:
                            c, n = GROUP_ORDER[i - 1]
                            k0, nb, _ = keys_of(c)
                            tile_drained(pe, ("pt", i - 1, 2))
                            tile_drained(pe, ("pt", i - 1, 3))
                            key = ("pv", i - 1)
                            ps = take(key)
                            for j in range(GRP):
                                for k in range(nb):
                                    ins = pe.matmul(ps[:, j * HD:(j + 1) * HD], ptb[:, j, k * P:(k + 1) * P],
                                                    kv[:, k0 + k, NKV * HD + n * HD:NKV * HD + (n + 1) * HD],
                                                    start=(k == 0), stop=(k == nb - 1))
                            done(ins, key)
                        for t in w[1:]:
                            stream_tile(t)
                    pe.wait_ge(ones_made, 1)
                    pe.wait_ge(cv_used, 16)
                    tile_drained(pe, ("v", NC - 2))
                    tile_drained(pe, ("v", NC - 1))
                    for g in range(9):
                        if g < 8:
                            h, s = ML_GROUPS[g]
                            n, lo = CHUNKS[s], BASE[s] * P
                            for d in range(2):
                                key = ("rb", g, d)
                                ps = take(key)
                                done(pe.matmul(ps[:, 0:n * P], sel_rows(4 * d + h), rrow[0:8, lo:lo + n * P], start=True, stop=True), key)
                            for sc in range(n):
                                key = ("st", g, sc)
                                ps = take(key)
                                done(pe.matmul(ps[:, 0:n * P], conv[:, 4 + h, lo + sc * P:lo + (sc + 1) * P],
                                               conv[:, h, lo:lo + n * P], start=True, stop=True), key)
                        if g == 0:
                            for c in range(NC):
                                pe.wait_ge(y_att, c + 1)
                                turn4(("yt", c, 0), lambda k: y[:, c, k * P:(k + 1) * P])
                        if g:
                            gg = g - 1
                            h, s = ML_GROUPS[gg]
                            n = CHUNKS[s]
                            tile_drained(pe, ("st", gg, n - 1))
                            for t in range(n):
                                key = ("nm", gg, t)
                                ps = take(key)
                                for d in range(2):
                                    ss = range(0, t + 1) if d == 0 else range(t, n)
                                    for sc in ss:
                                        ins = pe.matmul(ps[:, 256 * d:256 * d + MD + 1], sw_at(gg, d, n, sc, t, t + 1),
                                                        va[:, BASE[s] + sc, h, :], start=(sc == ss[0]), stop=(sc == ss[-1]))
                                done(ins, key)
                    s_ = UNIT["mem"] % SLOTS
                    mem = ring[:, s_ * 4096:(s_ + 1) * 4096].rearrange("p (m d) -> p m d", m=2 * MC)
                    wv2 = [unit_view("wo0", 512), unit_view("wo1", 512)]
                    for key in OUT_ORDER:
                        if key[0] == "yt":
                            c = key[1]
                            pe.wait_ge(y_ml, 7 if SEQ_OF[c] == 0 else 8)
                            turn4(key, lambda k: y[:, c, ATT + k * P:ATT + (k + 1) * P])
                        elif key[0] == "wo":
                            _, c, h = key
                            tile_drained(pe, ("yt", c, 1))
                            if c == 0 and h == 0:
                                tile_drained(pe, ("yt", NC - 2, 0))
                                tile_drained(pe, ("yt", NC - 1, 0))
                                unit_ready("wo0")
                                unit_ready("wo1")
                            product(key, 512, lambda k: xT[:, k, c * P:(c + 1) * P], lambda k: wv2[h][:, k, :])
                        else:
                            if key[1] == 0:
                                unit_ready("mem")
                            turn4(key, lambda m: mem[:, m, key[1] * P:(key[1] + 1) * P])
                    for k in range(KD):
                        tile_drained(pe, ("mt", k))
                    for q, keys in enumerate(QUARTERS):
                        pe.wait_ge(w_lo, q + 1)
                        whi, wlo = quarter_parts(q)
                        for i, key in enumerate(keys):
                            ps = take(key)
                            for k in range(KD):
                                for a, (wp, mp) in enumerate(((whi, memT_hi), (wlo, memT_hi), (whi, memT_lo))):
                                    start, stop = k == 0 and a == 0, k == KD - 1 and a == 2
                                    if key[0] == "km":
                                        ins = pe.matmul(ps[:, :], wp[:, k, i * P:(i + 1) * P], mp[:, k, :], start=start, stop=stop)
                            if key[0] == "vm":
                                for m in (2 * i, 2 * i + 1):
                                    o = 256 * (m % 2)
                                    for k in range(KD):
                                        for a, (wp, mp) in enumerate(((whi, memT_hi), (wlo, memT_hi), (whi, memT_lo))):
                                            ins = pe.matmul(ps[:, o:o + 256], mp[:, k, m * P:(m + 1) * P], wp[:, k, :],
                                                            start=k == 0 and a == 0, stop=k == KD - 1 and a == 2)
                            done(ins, key)
                    for c in range(NC):
                        pe.wait_ge(x_ready, c + 1)
                        for h in range(2):
                            turn4(("x2", c, h), lambda k: x[:, c, (4 * h + k) * P:(4 * h + k + 1) * P])
                    tile_drained(pe, ("x2", NC - 1, 0))
                    tile_drained(pe, ("x2", NC - 1, 1))
                    for j in range(KD):
                        name = "wq0" if j < 4 else "wq1"
                        unit_ready(name)
                        w = unit_view(name, 512)
                        for s in range(2):
                            lo = BASE[s] * P
                            product(("qx", j, s), SEQS[s], lambda k: w[:, k, (j % 4) * P:(j % 4 + 1) * P],
                                    lambda k: xT[:, k, lo:lo + SEQS[s]])
                    tile_drained(pe, ("qx", KD - 1, 0))
                    tile_drained(pe, ("qx", KD - 1, 1))

                    def cross_scores(i):
                        c, hp = X_ITEMS[i]
                        key = ("sx", i)
                        ps = take(key)
                        mo = SEQ_OF[c] * NMEM
                        for h in range(2):
                            for k in range(2):
                                j = 2 * (2 * hp + h) + k
                                ins = pe.matmul(ps[:, h * NMEM:(h + 1) * NMEM], qx[:, j, c * P:(c + 1) * P],
                                                km[:, j, mo:mo + NMEM], start=(k == 0), stop=(k == 1))
                        done(ins, key)

                    def cross_out(c):
                        if c == 0:
                            unit_ready("wx0")
                            unit_ready("wx1")
                        w2 = [unit_view("wx0", 512), unit_view("wx1", 512)]
                        for h in range(2):
                            product(("wx", c, h), 512, lambda k: xT[:, k, c * P:(c + 1) * P], lambda k: w2[h][:, k, :])

                    cross_scores(0)
                    cross_scores(1)
                    for i in range(12):
                        if i + 2 < 12:
                            cross_scores(i + 2)
                        pe.wait_ge(xp_ready, i + 1)
                        turn4(("px", i), lambda q: xp[:, i % 2, q * P:(q + 1) * P])
                        if i % 4 == 3:
                            cp = i // 4
                            tile_drained(pe, ("px", i - 1))
                            tile_drained(pe, ("px", i))
                            for m in range(4):
                                key = ("ox", cp, m)
                                ps = take(key)
                                for jj in range(2):
                                    j = 2 * m + jj
                                    for k in range(MC):
                                        ins = pe.matmul(ps[:, jj * 256:(jj + 1) * 256],
                                                        vm[:, SEQ_OF[2 * cp] * MC + k, j * P:(j + 1) * P],
                                                        xpt[:, j // 2, k, :], start=(k == 0), stop=(k == MC - 1))
                                done(ins, key)
                            if cp:
                                for m in range(4):
                                    tile_drained(pe, ("ox", cp - 1, m))
                                cross_out(2 * cp - 2)
                                cross_out(2 * cp - 1)
                    for m in range(4):
                        tile_drained(pe, ("ox", 2, m))
                    pe.wait_ge(router_loaded, 32)
                    rw = rw_t[:, :].rearrange("p (k e) -> p k e", k=KD)
                    for key in ROUTER_ORDER:
                        if key[0] == "wx":
                            if key[2] == 0:
                                cross_out(key[1])
                        elif key[0] == "x3":
                            _, c, h = key
                            pe.wait_ge(x_ready, NC + c + 1)
                            turn4(key, lambda k: x[:, c, (4 * h + k) * P:(4 * h + k + 1) * P])
                        elif key[0] == "rl":
                            c0, n = ROUTER_PARTS[key[1]]
                            for c in range(c0, c0 + n):
                                for h in range(2):
                                    tile_drained(pe, ("x3", c, h))
                            ps = take(key)
                            for k in range(KD):
                                ins = pe.matmul(ps[0:NE, 0:n * P], rw[:, k, :], xT[:, k, c0 * P:(c0 + n) * P],
                                                start=(k == 0), stop=(k == KD - 1))
                            done(ins, key)
                        else:
                            for i in range(3):
                                tile_drained(pe, ("rl", i))
                            ps = take(key)
                            for c in range(NC):
                                ins = pe.transpose(ps[:, c * NE:(c + 1) * NE], rrow[0:NE, c * P:(c + 1) * P], ident[0:NE, 0:NE])
                            done(ins, key)
                    pe.wait_ge(mask_ready, 1)
                    ps = take(("rank",))
                    pe.matmul(ps[:, 0:NS_], cst[:, C_STRICT:C_STRICT + P], r_m, start=True, stop=True)
                    done(pe.matmul(ps[:, NS_:2 * NS_], cst[:, C_ONES:C_ONES + P], r_m, start=True, stop=True), ("rank",))

                    pe.wait_ge(ids_ready, 1)
                    n_blocks = pe.value_load(r_nbi[0:1, 0:1], min_val=1, max_val=BLOCKS)
                    pe.sem_inc(g_filled, 1)
                    pe.sem_inc(u_filled, 1)
                    pe.sem_inc(y_filled, 1)
                    for bk in range(8):
                        pe.wait_ge(drained[bk], USES_BEFORE_EXPERTS[bk])

                    def turn_block():
                        for h in range(2):
                            for k in range(4):
                                q = 4 * h + k
                                ins = pe.transpose(banks[h][:, k * P:(k + 1) * P], xb[:, q * P:(q + 1) * P], ident)
                            ins.then_inc(xT_filled, 1)

                    wg = ring[:, 2 * 4096:3 * 4096].rearrange("p (k n) -> p k n", k=KD)
                    wu = ring[:, 0:4096].rearrange("p (k n) -> p k n", k=KD)
                    wd = ring[:, 4096:2 * 4096].rearrange("p (k n) -> p k n", k=4)
                    pe.wait_ge(x_loaded, 16)
                    turn_block()
                    with pe.Fori(0, n_blocks) as b:
                        pe.wait_ge(xT_ready, b + 1)
                        pe.wait_ge(g_loaded, 16 * b + 16)
                        pe.wait_ge(g_ready, b + 1)
                        for k in range(KD):
                            ins = pe.matmul(banks[2][:, :], xbT[:, k, :], wg[:, k, :], start=(k == 0), stop=(k == KD - 1))
                        ins.then_inc(g_filled, 1)
                        pe.wait_ge(u_loaded, 16 * b + 16)
                        pe.wait_ge(h_done, b + 1)
                        for h, bank, signal in ((0, 3, ul_filled), (1, 7, u_filled)):
                            for k in range(KD):
                                ins = pe.matmul(banks[bank][:, 0:256], xbT[:, k, :], wu[:, k, 256 * h:256 * h + 256],
                                                start=(k == 0), stop=(k == KD - 1))
                            ins.then_inc(signal, 1)
                        pe.wait_ge(hl_done, b + 1)
                        for k in range(2):
                            ins = pe.transpose(banks[4][:, k * P:(k + 1) * P], hb[:, k * P:(k + 1) * P], ident)
                        ins.then_inc(hTl_filled, 1)
                        pe.wait_ge(x_loaded, 16 * b + 32)
                        turn_block()
                        pe.wait_ge(h_done, b + 2)
                        for k in range(2, 4):
                            ins = pe.transpose(banks[3][:, k * P:(k + 1) * P], hb[:, k * P:(k + 1) * P], ident)
                        ins.then_inc(hT_filled, 1)
                        pe.wait_ge(d_loaded, 16 * b + 16)
                        pe.wait_ge(yl_ready, b + 1)
                        pe.wait_ge(yr_ready, b + 1)
                        pe.wait_ge(hTl_ready, b + 1)
                        for h in range(2):
                            for k in range(4):
                                if h == 0 and k == 2:
                                    pe.wait_ge(hT_ready, b + 1)
                                ins = pe.matmul(banks[5 + h][:, :], hbT[:, k, :], wd[:, k, 512 * h:512 * h + 512],
                                                start=(k == 0), stop=(k == 3))
                            ins.then_inc(y_filled, 1)
                    for c in range(NC):
                        pe.wait_ge(x_out, c + 1)
                        for h in range(2):
                            turn4(("xn", c, h), lambda k: x[:, c, (4 * h + k) * P:(4 * h + k + 1) * P])

            for s in layer_sems:
                nc.sync.sem_clear(s)
            nc.all_engine_barrier()

        with nc.Block() as end:
            @end.sync
            def _(sp):
                sp.wait_ge(out_stored, 16 * NC)


_INS = ["x_prompt", "x_sample", "mem_prompt", "mem_sample", "w_in", "gate_bias", "conv_w", "conv_b", "attn_sink",
        "attn_norm_g", "mlstm_norm_g", "w_out", "ln1_g", "ln1_b", "wq_mem", "wkv_mem", "wo_mem", "ln2_g", "ln2_b",
        "router_w", "router_bias", "w_gate", "w_up", "w_down", "ln3_g", "ln3_b"]


def kernel(**inputs):
    import concourse.bacc as _bacc
    from concourse.bass_utils import run_bass_kernel_spmd as _run

    nc = _bacc.Bacc("TRN2", target_bir_lowering=False, num_devices=1)
    arrays, args = {}, []
    for name in _INS:
        a = np.ascontiguousarray(inputs[name])
        arrays[f"in_{name}"] = a
        args.append(nc.dram_tensor(f"in_{name}", a.shape, mybir.dt.from_np(a.dtype), kind="ExternalInput").ap())
    arrays["in_consts"] = constants()
    args.append(nc.dram_tensor("in_consts", [P, C_ALL], F32, kind="ExternalInput").ap())
    outs = [nc.dram_tensor(f"out_{i}", [1, n, D], F32, kind="ExternalOutput").ap() for i, n in enumerate(SEQS)]
    build_program(nc, *args, *outs)
    r = _run(nc, [arrays], core_ids=[0])
    return tuple(r.results[0][f"out_{i}"] for i in range(2))
```
